# Optimizing a Trainium2 kernel written in Bass

```python
import jax, jax.numpy as jnp
from jax import lax
import numpy as np

D_MODEL = 1024
BATCH = 1
SEQ = 256
DEPTH = 2

FOURIER_GROUPS = 4
FOURIER_GROUP_DIM = 128
FOURIER_WIDTH = FOURIER_GROUPS * FOURIER_GROUP_DIM

DILATION_PATTERNS = ((128, 1), (512, 4), (2048, 16))
N_DIL_GROUPS = len(DILATION_PATTERNS)
HEADS_PER_GROUP = 4
HEAD_DIM = 64
N_ATTN_HEADS = N_DIL_GROUPS * HEADS_PER_GROUP
ATTN_WIDTH = N_ATTN_HEADS * HEAD_DIM
ATTN_OUT_WIDTH = HEADS_PER_GROUP * HEAD_DIM
Q_BLOCK = 128
ROPE_THETA = 10000.0

IN_COLS = FOURIER_WIDTH + 3 * ATTN_WIDTH + 2 * D_MODEL

FFN_DIM = 3584
N_EXPERTS = 8
TOP_K = 2
N_DENSE_LAYERS = (DEPTH + 1) // 2
N_MOE_LAYERS = DEPTH // 2

RMS_EPS = 1e-6
NEG_INF = -1e30

kernel_name = "hybrid_fourier_dilated_attn_moe_encoder"

def rms_norm(x, gain):
    xf = x.astype(jnp.float32)
    y = xf * lax.rsqrt(jnp.mean(xf * xf, axis=-1, keepdims=True) + RMS_EPS)
    return (y * gain.astype(jnp.float32)).astype(x.dtype)

def rope_tables(seq_len):
    half = HEAD_DIM // 2
    inv_freq = ROPE_THETA ** (-jnp.arange(half, dtype=jnp.float32) * 2.0 / HEAD_DIM)
    pos = jnp.arange(seq_len, dtype=jnp.float32)
    ang = pos[:, None] * inv_freq[None, :]
    return jnp.cos(ang), jnp.sin(ang)

def apply_rope(t, cos, sin):
    half = HEAD_DIM // 2
    tf = t.astype(jnp.float32)
    t1, t2 = tf[..., :half], tf[..., half:]
    c = cos[None, :, None, :]
    s = sin[None, :, None, :]
    return jnp.concatenate([t1 * c - t2 * s, t2 * c + t1 * s], axis=-1).astype(t.dtype)

def fourier_mix(u):
    b, s, _ = u.shape
    ug = u.reshape(b, s, FOURIER_GROUPS, FOURIER_GROUP_DIM).astype(jnp.float32)
    yf = jnp.fft.fft2(ug, axes=(1, 3), norm="ortho").real
    return yf.reshape(b, s, FOURIER_WIDTH).astype(u.dtype)

def dilated_window_attention(q, k, v, window, dilation):
    b, s, h, hd = q.shape
    half_span = window // (2 * dilation)
    offsets = dilation * jnp.arange(-half_span, half_span + 1)
    n_blk = s // Q_BLOCK
    q_blocks = q.reshape(b, n_blk, Q_BLOCK, h, hd).transpose(1, 0, 2, 3, 4)
    starts = jnp.arange(n_blk) * Q_BLOCK

    def one_block(args):
        q_blk, start = args
        pos = start + jnp.arange(Q_BLOCK)
        idx = pos[:, None] + offsets[None, :]
        valid = (idx >= 0) & (idx < s)
        idx_c = jnp.clip(idx, 0, s - 1)
        k_g = k[:, idx_c]
        v_g = v[:, idx_c]
        scores = jnp.einsum("bqhd,bqkhd->bhqk", q_blk, k_g).astype(jnp.float32)
        scores = jnp.where(valid[None, None], scores, NEG_INF)
        lse = jax.nn.logsumexp(scores, axis=-1)
        p = jnp.exp(scores - lse[..., None])
        out = jnp.einsum("bhqk,bqkhd->bqhd", p.astype(v.dtype), v_g)
        return out, lse.transpose(0, 2, 1)

    out, lse = lax.map(one_block, (q_blocks, starts))
    out = out.transpose(1, 0, 2, 3, 4).reshape(b, s, h, hd)
    lse = lse.transpose(1, 0, 2, 3).reshape(b, s, h)
    return out, lse

def swiglu(h, w1, w3, w2):
    return (jax.nn.silu(h @ w1) * (h @ w3)) @ w2

def moe_swiglu(h, w_router, b_router, w1, w3, w2):
    logits = (h @ w_router).astype(jnp.float32) + b_router.astype(jnp.float32)
    top_vals, top_idx = lax.top_k(logits, TOP_K)
    top_w = jax.nn.softmax(top_vals, axis=-1)
    combine = jnp.sum(jax.nn.one_hot(top_idx, N_EXPERTS, dtype=jnp.float32) * top_w[..., None], axis=-2)
    combine = combine.astype(h.dtype)
    out = jnp.zeros_like(h)
    for e in range(N_EXPERTS):
        out = out + combine[..., e:e + 1] * swiglu(h, w1[e], w3[e], w2[e])
    return out

def setup_inputs(seed: int = 0) -> dict:
    key = jax.random.key(seed)
    ks = jax.random.split(key, 20)
    f32 = jnp.float32

    def nrm(k, shape, fan_in):
        return jax.random.normal(k, shape, f32) * (fan_in ** -0.5)

    def gain(k, shape):
        return 1.0 + 0.05 * jax.random.normal(k, shape, f32)

    return {
        "x": jax.random.normal(ks[0], (BATCH, SEQ, D_MODEL), f32),
        "ln_mix": gain(ks[1], (DEPTH, D_MODEL)),
        "w_in": nrm(ks[2], (DEPTH, D_MODEL, IN_COLS), D_MODEL),
        "w_fourier": nrm(ks[3], (DEPTH, FOURIER_WIDTH, D_MODEL), FOURIER_WIDTH),
        "w_attn": nrm(ks[4], (DEPTH, ATTN_OUT_WIDTH, D_MODEL), ATTN_OUT_WIDTH),
        "w_out": nrm(ks[5], (DEPTH, D_MODEL, D_MODEL), D_MODEL),
        "ln_ffn": gain(ks[6], (DEPTH, D_MODEL)),
        "dense_w1": nrm(ks[7], (N_DENSE_LAYERS, D_MODEL, FFN_DIM), D_MODEL),
        "dense_w3": nrm(ks[8], (N_DENSE_LAYERS, D_MODEL, FFN_DIM), D_MODEL),
        "dense_w2": nrm(ks[9], (N_DENSE_LAYERS, FFN_DIM, D_MODEL), FFN_DIM),
        "router_w": nrm(ks[10], (N_MOE_LAYERS, D_MODEL, N_EXPERTS), D_MODEL),
        "router_b": 0.01 * jax.random.normal(ks[11], (N_MOE_LAYERS, N_EXPERTS), f32),
        "moe_w1": nrm(ks[12], (N_MOE_LAYERS, N_EXPERTS, D_MODEL, FFN_DIM), D_MODEL),
        "moe_w3": nrm(ks[13], (N_MOE_LAYERS, N_EXPERTS, D_MODEL, FFN_DIM), D_MODEL),
        "moe_w2": nrm(ks[14], (N_MOE_LAYERS, N_EXPERTS, FFN_DIM, D_MODEL), FFN_DIM),
        "ln_final": gain(ks[15], (D_MODEL,)),
    }

def reference(x, ln_mix, w_in, w_fourier, w_attn, w_out, ln_ffn, dense_w1, dense_w3, dense_w2,
              router_w, router_b, moe_w1, moe_w3, moe_w2, ln_final):
    b, s, _ = x.shape
    cos, sin = rope_tables(s)
    q_scale = HEAD_DIM ** -0.5
    split_points = np.cumsum([FOURIER_WIDTH, ATTN_WIDTH, ATTN_WIDTH, ATTN_WIDTH, D_MODEL]).tolist()

    for layer in range(DEPTH):
        h = rms_norm(x, ln_mix[layer])
        proj = h @ w_in[layer]
        u_f, q, k, v, gate_f, gate_a = jnp.split(proj, split_points, axis=-1)

        y_f = fourier_mix(u_f) @ w_fourier[layer]

        q = apply_rope(q.reshape(b, s, N_ATTN_HEADS, HEAD_DIM), cos, sin) * q_scale
        k = apply_rope(k.reshape(b, s, N_ATTN_HEADS, HEAD_DIM), cos, sin)
        v = v.reshape(b, s, N_ATTN_HEADS, HEAD_DIM)
        outs, lses = [], []
        for g, (window, dilation) in enumerate(DILATION_PATTERNS):
            hs = slice(g * HEADS_PER_GROUP, (g + 1) * HEADS_PER_GROUP)
            o_g, lse_g = dilated_window_attention(q[:, :, hs], k[:, :, hs], v[:, :, hs], window, dilation)
            outs.append(o_g)
            lses.append(lse_g)
        o_all = jnp.stack(outs, axis=0).astype(jnp.float32)
        alpha = jax.nn.softmax(jnp.stack(lses, axis=0), axis=0)
        o_att = jnp.einsum("gbsh,gbshd->bshd", alpha, o_all).astype(x.dtype)
        y_a = o_att.reshape(b, s, ATTN_OUT_WIDTH) @ w_attn[layer]

        g_f = jax.nn.sigmoid(gate_f.astype(jnp.float32)).astype(x.dtype)
        g_a = jax.nn.sigmoid(gate_a.astype(jnp.float32)).astype(x.dtype)
        x = x + (g_f * y_f + g_a * y_a) @ w_out[layer]

        h2 = rms_norm(x, ln_ffn[layer])
        if layer % 2 == 0:
            i = layer // 2
            x = x + swiglu(h2, dense_w1[i], dense_w3[i], dense_w2[i])
        else:
            i = layer // 2
            x = x + moe_swiglu(h2, router_w[i], router_b[i], moe_w1[i], moe_w3[i], moe_w2[i])

    return rms_norm(x, ln_final)


_drawn_inputs = setup_inputs


def setup_inputs(seed=0):
    import zlib

    import numpy as np

    out = dict(_drawn_inputs(seed))
    spreads = {}
    factors = {}
    for name, (base, spread) in spreads.items():
        noise = np.random.default_rng([zlib.crc32(name.encode()), seed]).standard_normal(out[name].shape)
        drawn = base * np.exp(spread * noise) if base else spread * noise
        out[name] = __import__('jax').numpy.asarray(drawn.astype(out[name].dtype))
    for name, factor in factors.items():
        out[name] = (out[name] * factor).astype(out[name].dtype)
    return out
```

```python
from contextlib import ExitStack

import concourse.bass as bass
from concourse import mybir

F32 = mybir.dt.float32
F32R = mybir.dt.float32r
I32 = mybir.dt.int32
ALU = mybir.AluOpType
ACT = mybir.ActivationFunctionType
AX_X = mybir.AxisListType.X

P = 128
D = 1024
SEQ = 256
NT = SEQ // P
KD = D // P
NB = 512
FG = 4
HG = 4
HD = 64
NG = 3
AW = NG * HG * HD
FFN = 3584
NSTEP = FFN // NB
NE = 8
RAW = 6
SPL = 3
BLK = 2048
MIX = 26
FF = 6 * NSTEP
DENSE0 = MIX
MIX1 = MIX + FF
MOE0 = 2 * MIX + FF
EPS = 1e-6
QS = HD ** -0.5
NPROD = 20


def build(nc, x_in, ln_mix, w_in, w_fourier, w_attn, w_out, ln_ffn, dense_w1, dense_w3, dense_w2,
          router_w, router_b, moe_w1, moe_w3, moe_w2, ln_final,
          c_ident, c_dftpos, c_dftch, c_mask, c_rope, c_iota, c_before, out):
    with ExitStack() as ctx:
        def sb(name, shape, dt=F32):
            return ctx.enter_context(nc.sbuf_tensor(name, shape, dt))

        def sem(name):
            return ctx.enter_context(nc.semaphore(name))

        raw = sb("raw", [P, RAW, BLK])
        whi = sb("whi", [P, SPL, BLK], F32R)
        wlo = sb("wlo", [P, SPL, BLK], F32R)
        x = sb("x", [P, NT, D])
        h = sb("h", [P, NT, D])
        hT_hi = sb("hT_hi", [P, KD * SEQ], F32R)
        hT_lo = sb("hT_lo", [P, KD * SEQ], F32R)
        aT_hi = sb("aT_hi", [P, NT * NB], F32R)
        aT_lo = sb("aT_lo", [P, NT * NB], F32R)
        ho = sb("ho", [P, NT, NB])
        qg = sb("qg", [P, NT, 2 * D])
        v = sb("v", [P, NT, AW])
        qkT = sb("qkT", [P, 3072])
        att = sb("att", [P, 3072])
        os_hi = sb("os_hi", [P, D], F32R)
        os_lo = sb("os_lo", [P, D], F32R)
        o = sb("o", [P, NT, HG * HD])
        ident = sb("ident", [P, P])
        dftch = sb("dftch", [P, 2, P])
        mask = sb("mask", [P, 4 * SEQ])
        rope = sb("rope", [P, NT, 2, HD])
        iota = sb("iota", [P, P])
        before = sb("before", [P, P])
        ones = sb("ones", [P, P])
        rw = sb("rw", [P, KD, NE])
        rb = sb("rb", [P, NE])
        sel = sb("sel", [P, NT, P])
        selT = sb("selT", [P, SEQ], F32R)
        ssq = sb("ssq", [P, NT])
        var = sb("var", [P, NT])
        std = sb("std", [P, NT])
        rstd = sb("rstd", [P, NT])
        mx = sb("mx", [P, 2])
        nmx = sb("nmx", [P, 2])
        den = sb("den", [P, 16])
        rden = sb("rden", [P, 16])
        rt = sb("rt", [P, NT, 10, NE])
        r1 = sb("r1", [P, NT, 8])
        comb = sb("comb", [P, NT, 2 * NE + 1])
        pos = sb("pos", [P, NT, 2 * NE + 1])
        njobs_f = sb("njobs_f", [P, 4])
        njobs_i = sb("njobs_i", [P, 1], I32)

        ps = ctx.enter_context(nc.psum_tensor("ps", [P, 8, NB], F32))

        gain = att[:, 0:D]
        fab = att[:, 0:FG * NB].rearrange("p (g c) -> p g c", g=FG)
        s_sb = [att[:, 0:AW], att[:, AW:2 * AW]]
        p_sb = att[:, 2 * AW:3 * AW]
        pT = att[:, 3 * AW:4 * AW]
        dftpos = qkT[:, 0:NT * NB].rearrange("p (t c) -> p t c", t=NT)
        qkTc = qkT[:, :].rearrange("p (c s) -> p c s", c=12)
        routT = qg[:, :, :].rearrange("p a b -> p (a b)")[:, 0:KD * SEQ].rearrange("p (k s) -> p k s", k=KD)
        Y0 = 6
        psY = ps[:, 6:8, :].rearrange("p b c -> p (b c)")
        psT = ps[:, 4:6, :].rearrange("p b c -> p (b c)")
        ps23 = ps[:, 2:4, :].rearrange("p b c -> p (b c)")

        x_landed = sem("x_landed")
        const_landed = sem("const_landed")
        gain_landed = sem("gain_landed")
        dft_landed = sem("dft_landed")
        raw_landed = [sem(f"raw_landed{i}") for i in range(RAW)]
        hi_ready = sem("hi_ready")
        lo_ready = sem("lo_ready")
        w_used = sem("w_used")
        init_done = sem("init_done")
        var_ready = sem("var_ready")
        std_ready = sem("std_ready")
        norm_step = sem("norm_step")
        h_ready = sem("h_ready")
        hT_full = sem("hT_full")
        hT_hi_done = sem("hT_hi_done")
        hT_lo_done = sem("hT_lo_done")
        proj_evac = sem("proj_evac")
        rope_step = sem("rope_step")
        rope_done = sem("rope_done")
        qkT_full = sem("qkT_full")
        qkT_evac = sem("qkT_evac")
        fa_full = sem("fa_full")
        fa_evac = sem("fa_evac")
        fb_full = sem("fb_full")
        fb_hi = sem("fb_hi")
        fb_lo = sem("fb_lo")
        sc_full = sem("sc_full")
        sc_used = sem("sc_used")
        nmx_ready = sem("nmx_ready")
        p_ready = sem("p_ready")
        pT_full = sem("pT_full")
        pT_evac_a = sem("pT_evac_a")
        pT_evac_d = sem("pT_evac_d")
        pv_full = sem("pv_full")
        rden_ready = sem("rden_ready")
        o_done = sem("o_done")
        oT_full = sem("oT_full")
        oT_hi = sem("oT_hi")
        oT_lo = sem("oT_lo")
        zf_done = sem("zf_done")
        za_done = sem("za_done")
        z_ready = sem("z_ready")
        x_done = sem("x_done")
        silu_done = sem("silu_done")
        act_ready = sem("act_ready")
        aT_full = sem("aT_full")
        aT_hi_done = sem("aT_hi_done")
        aT_lo_done = sem("aT_lo_done")
        y_full = sem("y_full")
        y_added = sem("y_added")
        rT_full = sem("rT_full")
        rT_evac = sem("rT_evac")
        logit_full = sem("logit_full")
        exp_ready = sem("exp_ready")
        route_step = sem("route_step")
        mask_ready = sem("mask_ready")
        rank_full = sem("rank_full")
        njobs_ready = sem("njobs_ready")
        sel_ready = sem("sel_ready")
        g_full = sem("g_full")
        g_hi = sem("g_hi")
        g_lo = sem("g_lo")
        yj_hi = sem("yj_hi")
        yj_lo = sem("yj_lo")
        selT_full = sem("selT_full")
        selT_ready = sem("selT_ready")
        scat_full = sem("scat_full")
        scat_added = sem("scat_added")
        out_done = sem("out_done")

        def proj_bank(q):
            return q % 4 if q < 12 else q % 2

        def pv_out(u):
            return ps[:, 2 + u % 2 if u < 6 else u, 0:HD]

        def k_rows(w):
            return w.rearrange("(k p) n -> p k n", p=P)

        def mix_src(L, m):
            wi = k_rows(w_in[L])
            if m < 10:
                return wi[:, 4 * (m % 2):4 * (m % 2) + 4, NB * (m // 2):NB * (m // 2) + NB], 4
            if m == 10:
                return wi[:, :, 2560:2816], 8
            if m < 19:
                a = 2816 + NB * ((m - 11) // 2)
                half = (m - 11) % 2
                return wi[:, 4 * half:4 * half + 4, a:a + NB], 4
            if m < 21:
                return k_rows(w_fourier[L])[:, 2 * (m - 19):2 * (m - 19) + 2, :], 2
            if m == 21:
                return k_rows(w_attn[L]), 2
            return k_rows(w_out[L])[:, 2 * (m - 22):2 * (m - 22) + 2, :], 2

        def wblock(buf, b_static, n, chunks):
            return buf[:, b_static % n, :].rearrange("p (k c) -> p k c", k=chunks)

        block = ctx.enter_context(nc.Block())

        @block.sync
        def _(sp):
            def load(b, b_static, src, chunks, first=False):
                if not first:
                    sp.wait_ge(lo_ready, b - RAW + 1)
                sp.dma_start(wblock(raw, b_static, RAW, chunks), src).then_inc(raw_landed[b_static % RAW], 16)

            def load_gain(src):
                sp.dma_start(gain, src.partition_broadcast(P)).then_inc(gain_landed, 16)

            sp.dma_start(x[:], x_in.rearrange("b (t p) d -> p (b t) d", p=P)).then_inc(x_landed, 16)
            load_gain(ln_mix[0])
            for L in range(2):
                base = 0 if L == 0 else MIX1
                if L == 1:
                    sp.wait_ge(h_ready, 4)
                    load_gain(ln_mix[1])
                    sp.wait_ge(pv_full, 8)
                sp.dma_start(dftpos, c_dftpos).then_inc(dft_landed, 16)
                for m in range(MIX):
                    src, chunks = mix_src(L, m)
                    load(base + m, base + m, src, chunks, first=base + m < RAW)
                sp.wait_ge(pv_full, 8 * L + 8)
                load_gain(ln_ffn[L])
                if L == 0:
                    w1, w3, w2 = k_rows(dense_w1[0]), k_rows(dense_w3[0]), k_rows(dense_w2[0])
                    for i in range(4):
                        w = w1 if i < 2 else w3
                        load(DENSE0 + i, DENSE0 + i, w[:, 4 * (i % 2):4 * (i % 2) + 4, 0:NB], 4)
                    with sp.Fori(1, NSTEP) as n:
                        for i in range(6):
                            s = DENSE0 + 4 + i
                            if i < 4:
                                w = w1 if i < 2 else w3
                                src = w[:, 4 * (i % 2):4 * (i % 2) + 4, bass.ds(n * NB, NB)]
                            else:
                                src = w2[:, bass.ds(4 * n - 4, 4), NB * (i - 4):NB * (i - 4) + NB]
                            load(DENSE0 - 2 + 6 * n + i, s, src, 4)
                    for i in range(2):
                        b = DENSE0 + 6 * NSTEP - 2 + i
                        load(b, b, w2[:, 4 * NSTEP - 4:4 * NSTEP, NB * i:NB * i + NB], 4)

            def load_expert(job, e):
                w1 = moe_w1[0][bass.ds(e, 1)].rearrange("e (k p) n -> p (e k) n", p=P)
                w3 = moe_w3[0][bass.ds(e, 1)].rearrange("e (k p) n -> p (e k) n", p=P)
                w2 = moe_w2[0][bass.ds(e, 1)].rearrange("e (k p) n -> p (e k) n", p=P)
                for i in range(FF):
                    n, q = divmod(i + 2, 6)
                    if i < 4:
                        n, q = 0, i
                    if i >= FF - 2:
                        n, q = NSTEP, 4 + i - (FF - 2)
                    if q < 4:
                        w = w1 if q < 2 else w3
                        src = w[:, 4 * (q % 2):4 * (q % 2) + 4, NB * n:NB * n + NB]
                    else:
                        src = w2[:, 4 * n - 4:4 * n, NB * (q - 4):NB * (q - 4) + NB]
                    load(FF * job + (MOE0 + i), MOE0 + i, src, 4)

            with sp.Fori(0, NE) as e:
                load_expert(e, e)
            sp.wait_ge(njobs_ready, 1)
            n_jobs = sp.value_load(njobs_i[0:1, 0:1], min_val=NE, max_val=2 * NE)
            with sp.If(n_jobs > NE):
                with sp.Fori(0, NE) as e2:
                    load_expert(e2 + NE, e2)
            sp.wait_ge(h_ready, 8)
            load_gain(ln_final)
            for t in range(NT):
                sp.wait_ge(h_ready, 9 + t)
                sp.dma_start(out[0, P * t:P * t + P, :], h[:, t, :]).then_inc(out_done, 16)
            sp.wait_ge(out_done, 32)

        @block.scalar
        def _(act):
            def split_loop(s, landed_add, used_add):
                act.wait_ge(raw_landed[s % RAW], landed_add + (16 * (s // RAW) + 16))
                act.wait_ge(w_used, used_add + (s - SPL + 1))
                nc.scalar.copy(whi[:, s % SPL, :], raw[:, s % RAW, :]).then_inc(hi_ready, 1)

            def norm_std(N):
                for t in range(NT):
                    act.wait_ge(var_ready, 2 * N + t + 1)
                    nc.scalar.activation(std[:, t:t + 1], var[:, t:t + 1], ACT.Sqrt).then_inc(std_ready, 1)

            def rows_T_hi(K):
                for r in range(4):
                    t, c = divmod(r, 2)
                    act.wait_ge(hT_full, 4 * K + r + 1)
                    dst = hT_hi[:, :].rearrange("p (k s) -> p k s", k=KD)[:, 4 * c:4 * c + 4, P * t:P * t + P]
                    nc.scalar.copy(dst, ps[:, 4 + r % 2, :].rearrange("p (k s) -> p k s", k=4)) \
                        .then_inc(hT_hi_done, 1)

            for dst, src in ((ident[:], c_ident), (dftch[:], c_dftch), (mask[:], c_mask), (rope[:], c_rope),
                             (iota[:], c_iota), (before[:], c_before), (rw[:], k_rows(router_w[0])),
                             (rb[:], router_b[0].partition_broadcast(P))):
                act.dma_start(dst, src).then_inc(const_landed, 16)

            def mixer(L):
                base = 0 if L == 0 else MIX1

                def split(m):
                    split_static(base + m)

                def evac(q):
                    n, t = divmod(q, 2)
                    last = 2 * n + 1 if n < 5 else 2 * n
                    act.wait_ge(w_used, base + last + 1)
                    src = ps[:, proj_bank(q), :]
                    if n == 0:
                        nc.scalar.copy(ho[:, t, :], src).then_inc(proj_evac, 1)
                    elif n < 4:
                        nc.scalar.copy(qg[:, t, NB * (n - 1):NB * n], src).then_inc(proj_evac, 1)
                    elif n == 4:
                        nc.scalar.copy(v[:, t, 0:NB], src).then_inc(proj_evac, 1)
                    elif n == 5:
                        nc.scalar.copy(v[:, t, NB:AW], src[:, 0:AW - NB]).then_inc(proj_evac, 1)
                    else:
                        nc.scalar.activation(qg[:, t, NB * (n - 6):NB * (n - 5)], src, ACT.Sigmoid) \
                            .then_inc(proj_evac, 1)

                def qk_evac(i):
                    part, t = divmod(i, 2)
                    act.wait_ge(qkT_full, 4 * L + i + 1)
                    nc.scalar.copy(qkTc[:, 6 * part:6 * part + 6, P * t:P * t + P],
                                   psT[:, 0:AW].rearrange("p (c s) -> p c s", c=6)).then_inc(qkT_evac, 1)

                def softmax_exp(u):
                    act.wait_ge(nmx_ready, 8 * L + u + 1)
                    if 8 * L + u >= 1:
                        act.wait_ge(pT_full, 8 * L + u)
                    nc.scalar.activation(p_sb, s_sb[u % 2], ACT.Exp, bias=nmx[:, u % 2:u % 2 + 1], scale=QS,
                                         accum_out=den[:, 8 * L + u:8 * L + u + 1]).then_inc(p_ready, 1)

                def pT_evac(u):
                    act.wait_ge(pT_full, 8 * L + u + 1)
                    if 8 * L + u >= 1:
                        act.wait_ge(pv_full, 8 * L + u)
                    nc.scalar.copy(pT[:, 0:NB], psT[:, 0:NB]).then_inc(pT_evac_a, 1)

                norm_std(2 * L)
                rows_T_hi(0 if L == 0 else 3)
                for n in range(5):
                    split(2 * n + 2)
                    if n == 4:
                        qk_evac(0)
                    split(2 * n + 3)
                    if n == 4:
                        qk_evac(1)
                    evac(2 * n)
                    evac(2 * n + 1)
                    if n == 3:
                        for i in range(2):
                            act.wait_ge(fb_full, 2 * L + i + 1)
                            nc.scalar.copy(aT_hi[:, NB * i:NB * i + NB], ps[:, 6 + i, :]).then_inc(fb_hi, 1)
                qk_evac(2)
                evac(10)
                evac(11)
                qk_evac(3)
                for i in range(9):
                    split(12 + i)
                    if i >= 2 and i % 2 == 0:
                        evac(12 + i - 2)
                        evac(12 + i - 1)
                    if i < 8:
                        softmax_exp(i)
                    if i >= 1:
                        pT_evac(i - 1)
                split(21)
                split(22)
                split(23)
                act.wait_ge(oT_full, L + 1)
                nc.scalar.copy(os_hi[:, 0:NB], ps[:, 4, :]).then_inc(oT_hi, 1)
                split(24)
                rows_T_hi(1 if L == 0 else 4)
                split(25)
                split(26)
                split(27)

            def split_static(b):
                act.wait_ge(raw_landed[b % RAW], 16 * (b // RAW) + 16)
                if b >= SPL:
                    act.wait_ge(w_used, b - SPL + 1)
                nc.scalar.copy(whi[:, b % SPL, :], raw[:, b % RAW, :]).then_inc(hi_ready, 1)

            split_static(0)
            split_static(1)
            mixer(0)

            norm_std(1)
            rows_T_hi(2)
            split_static(DENSE0 + 2)
            split_static(DENSE0 + 3)

            def dense_silu(used):
                act.wait_ge(w_used, used)
                for t in range(NT):
                    nc.scalar.activation(ho[:, t, :], ps[:, t, :], ACT.Silu).then_inc(silu_done, 1)

            def dense_hiT(k):
                act.wait_ge(aT_full, k)
                nc.scalar.copy(aT_hi[:], psT).then_inc(aT_hi_done, 1)

            split_static(DENSE0 + 4)
            split_static(DENSE0 + 5)
            dense_silu(DENSE0 + 4)
            with act.Fori(0, NSTEP - 1) as n:
                for i in range(2, 6):
                    split_loop(DENSE0 + 4 + i, 16 * n, 6 * n)
                    if i == 2:
                        dense_hiT(n + 1)
                    if i == 5:
                        dense_silu(n * 6 + (DENSE0 + 8))
                for i in range(6, 8):
                    split_loop(DENSE0 + 4 + i, 16 * n, 6 * n)
            split_static(MIX1)
            dense_hiT(NSTEP)
            split_static(MIX1 + 1)
            mixer(1)

            norm_std(3)
            for r in range(4):
                t, c = divmod(r, 2)
                act.wait_ge(rT_full, r + 1)
                nc.scalar.copy(routT[:, 4 * c:4 * c + 4, P * t:P * t + P],
                               ps[:, 4 + r % 2, :].rearrange("p (k s) -> p k s", k=4)).then_inc(rT_evac, 1)
            act.wait_ge(exp_ready, 1)
            nc.scalar.activation(r1[:, :, 3:4], r1[:, :, 2:3], ACT.Exp).then_inc(exp_ready, 1)
            act.wait_ge(njobs_ready, 1)
            n_jobs = act.value_load(njobs_i[0:1, 0:1], min_val=NE, max_val=2 * NE)

            def gather_hi(k):
                act.wait_ge(g_full, k)
                nc.scalar.copy(hT_hi[:, 0:D], ps23).then_inc(g_hi, 1)

            gather_hi(1)
            with act.Fori(0, n_jobs) as j:
                l16, u42, u7 = act.snap(j * (16 * FF // RAW)), act.snap(j * FF), act.snap(j * NSTEP)

                def split(i):
                    split_loop(MOE0 + i, l16, u42)

                def silu(n):
                    act.wait_ge(w_used, u42 + (MOE0 + (4 if n == 0 else 6 * n + 2)))
                    nc.scalar.activation(ho[:, 0, :], ps[:, 0, :], ACT.Silu).then_inc(silu_done, 1)

                def hiT(n):
                    act.wait_ge(aT_full, u7 + (NSTEP + n + 1))
                    nc.scalar.copy(aT_hi[:, 0:NB], ps[:, 4, :]).then_inc(aT_hi_done, 1)

                for i in range(2, 6):
                    split(i)
                silu(0)
                for n in range(1, NSTEP):
                    s = 6 * n - 2
                    split(s + 2)
                    hiT(n - 1)
                    if n == 2:
                        act.wait_ge(selT_full, j + 1)
                        nc.scalar.copy(selT[:], ps[:, 5, 0:SEQ]).then_inc(selT_ready, 1)
                    split(s + 3)
                    split(s + 4)
                    split(s + 5)
                    silu(n)
                    split(s + 6)
                    split(s + 7)
                hiT(NSTEP - 1)
                gather_hi(j + 2)
                with act.If(j + 1 < n_jobs):
                    split(FF)
                    split(FF + 1)
                act.wait_ge(w_used, u42 + (MOE0 + FF))
                nc.scalar.copy(os_hi[:], psY).then_inc(yj_hi, 1)
            norm_std(4)

        @block.gpsimd
        def _(pool):
            nc.gpsimd.memset(ones[:], 1.0).then_inc(init_done, 1)
            nc.gpsimd.memset(selT[:].bitcast(F32), 0.0).then_inc(init_done, 1)
            nc.gpsimd.memset(comb[:], 0.0).then_inc(init_done, 1)
            pool.wait_ge(const_landed, 16 * 8)
            tmp_a = h[:, 0, 0:AW].rearrange("p (h d) -> p h d", d=HD)
            tmp_b = h[:, 1, 0:AW].rearrange("p (h d) -> p h d", d=HD)
            half = HD // 2
            step = 0
            for L in range(2):
                for i in range(4):
                    part, t = divmod(i, 2)
                    pool.wait_ge(proj_evac, NPROD * L + (6 if part == 0 else 8))
                    t_in = qg[:, t, AW * part:AW * part + AW].rearrange("p (h d) -> p h d", d=HD)
                    nh = AW // HD
                    cos = rope[:, t, 0:1, :].broadcast_to([P, nh, HD])
                    nsin = rope[:, t, 1:2, 0:half].broadcast_to([P, nh, half])
                    psin = rope[:, t, 1:2, half:HD].broadcast_to([P, nh, half])
                    if step:
                        pool.wait_ge(rope_done, 4 * L + i)
                    nc.gpsimd.tensor_tensor(tmp_a, t_in, cos, ALU.mult).then_inc(rope_step, 1)
                    nc.gpsimd.tensor_tensor(tmp_b[:, :, 0:half], t_in[:, :, half:HD], nsin, ALU.mult) \
                        .then_inc(rope_step, 1)
                    nc.gpsimd.tensor_tensor(tmp_b[:, :, half:HD], t_in[:, :, 0:half], psin, ALU.mult) \
                        .then_inc(rope_step, 1)
                    step += 3
                    pool.wait_ge(rope_step, step)
                    nc.gpsimd.tensor_tensor(t_in, tmp_a, tmp_b, ALU.add).then_inc(rope_done, 1)

        @block.vector
        def _(dve):
            def split_static(b):
                dve.wait_ge(hi_ready, b + 1)
                nc.vector.tensor_tensor(wlo[:, b % SPL, :], raw[:, b % RAW, :],
                                        whi[:, b % SPL, :].bitcast(F32), ALU.subtract).then_inc(lo_ready, 1)

            def split_loop(s, add):
                dve.wait_ge(hi_ready, add + (s + 1))
                nc.vector.tensor_tensor(wlo[:, s % SPL, :], raw[:, s % RAW, :],
                                        whi[:, s % SPL, :].bitcast(F32), ALU.subtract).then_inc(lo_ready, 1)

            norm_steps = [0]

            def norm(N):
                for t in range(NT):
                    nc.vector.tensor_tensor_reduce(h[:, t, :], x[:, t, :], x[:, t, :], 1.0, 0.0, ALU.mult, ALU.add,
                                                   ssq[:, t:t + 1]).then_inc(norm_step, 1)
                for t in range(NT):
                    norm_steps[0] += 1
                    dve.wait_ge(norm_step, norm_steps[0])
                    nc.vector.tensor_scalar(var[:, t:t + 1], ssq[:, t:t + 1], 1.0 / D, EPS, ALU.mult, ALU.add) \
                        .then_inc(var_ready, 1)
                dve.wait_ge(gain_landed, 16 * N + 16)
                for t in range(NT):
                    dve.wait_ge(std_ready, 2 * N + t + 1)
                    nc.vector.reciprocal(rstd[:, t:t + 1], std[:, t:t + 1]).then_inc(norm_step, 1)
                    norm_steps[0] += 1
                    dve.wait_ge(norm_step, norm_steps[0])
                    nc.vector.scalar_tensor_tensor(h[:, t, :], x[:, t, :], rstd[:, t:t + 1], gain,
                                                   ALU.mult, ALU.mult).then_inc(h_ready, 1)

            def rows_T_lo(K):
                for r in range(4):
                    t, c = divmod(r, 2)
                    dve.wait_ge(hT_hi_done, 4 * K + r + 1)
                    view = lambda buf: buf.rearrange("p (k s) -> p k s", k=KD)[:, 4 * c:4 * c + 4, P * t:P * t + P]
                    nc.vector.tensor_tensor(view(hT_lo[:, :]), ps[:, 4 + r % 2, :].rearrange("p (k s) -> p k s", k=4),
                                            view(hT_hi[:, :].bitcast(F32)), ALU.subtract).then_inc(hT_lo_done, 1)

            def mixer(L):
                base = 0 if L == 0 else MIX1

                def split(m):
                    split_static(base + m)

                def row_max(u):
                    t = u // HG
                    dve.wait_ge(sc_full, 8 * L + u + 1)
                    if 8 * L + u >= 2:
                        dve.wait_ge(p_ready, 8 * L + u - 1)
                    nc.vector.tensor_tensor_reduce(s_sb[u % 2], psY[:, 0:AW], mask[:, SEQ * t:SEQ * t + AW],
                                                   1.0, -3.0e38, ALU.add, ALU.max, mx[:, u % 2:u % 2 + 1]) \
                        .then_inc(sc_used, 1)
                    dve.wait_ge(sc_used, 8 * L + u + 1)
                    nc.vector.tensor_scalar(nmx[:, u % 2:u % 2 + 1], mx[:, u % 2:u % 2 + 1], -QS, None, ALU.mult) \
                        .then_inc(nmx_ready, 1)

                def pT_evac(u):
                    dve.wait_ge(pT_full, 8 * L + u + 1)
                    if 8 * L + u >= 1:
                        dve.wait_ge(pv_full, 8 * L + u)
                    nc.vector.tensor_copy(pT[:, NB:AW], psT[:, NB:AW]).then_inc(pT_evac_d, 1)

                def normalise(u):
                    t, j = divmod(u, HG)
                    i = 8 * L + u
                    nc.vector.reciprocal(rden[:, i:i + 1], den[:, i:i + 1]).then_inc(rden_ready, 1)
                    dve.wait_ge(pv_full, i + 1)
                    dve.wait_ge(rden_ready, i + 1)
                    nc.vector.tensor_scalar(o[:, t, HD * j:HD * j + HD], pv_out(u),
                                            rden[:, i:i + 1], None, ALU.mult).then_inc(o_done, 1)

                norm(2 * L)
                if L == 0:
                    dve.wait_ge(const_landed, 16 * 8)
                rows_T_lo(0 if L == 0 else 3)
                for n in range(5):
                    split(2 * n + 2)
                    split(2 * n + 3)
                    if n == 2:
                        for g in range(FG):
                            dve.wait_ge(fa_full, FG * L + g + 1)
                            nc.vector.tensor_copy(fab[:, g, :], ps[:, 6 + g % 2, :]).then_inc(fa_evac, 1)
                    if n == 3:
                        for i in range(2):
                            dve.wait_ge(fb_hi, 2 * L + i + 1)
                            nc.vector.tensor_tensor(aT_lo[:, NB * i:NB * i + NB], ps[:, 6 + i, :],
                                                    aT_hi[:, NB * i:NB * i + NB].bitcast(F32), ALU.subtract) \
                                .then_inc(fb_lo, 1)
                for i in range(9):
                    split(12 + i)
                    if i < 8:
                        row_max(i)
                    if i >= 1:
                        pT_evac(i - 1)
                    if i >= 2:
                        normalise(i - 2)
                split(21)
                normalise(7)
                split(22)
                split(23)
                dve.wait_ge(oT_hi, L + 1)
                nc.vector.tensor_tensor(os_lo[:, 0:NB], ps[:, 4, :], os_hi[:, 0:NB].bitcast(F32), ALU.subtract) \
                    .then_inc(oT_lo, 1)
                dve.wait_ge(w_used, base + 21)
                for t in range(NT):
                    for c in range(2):
                        nc.vector.tensor_tensor(h[:, t, NB * c:NB * c + NB], ps[:, 2 * t + c, :],
                                                qg[:, t, NB * c:NB * c + NB], ALU.mult).then_inc(zf_done, 1)
                split(24)
                dve.wait_ge(w_used, base + 22)
                for t in range(NT):
                    for c in range(2):
                        i = 4 * L + 2 * t + c
                        if i >= 2:
                            dve.wait_ge(z_ready, i - 1)
                        nc.vector.tensor_tensor(ho[:, c, :], ps[:, 4 + 2 * t + c, :],
                                                qg[:, t, D + NB * c:D + NB * c + NB], ALU.mult).then_inc(za_done, 1)
                        dve.wait_ge(za_done, i + 1)
                        dve.wait_ge(zf_done, i + 1)
                        nc.vector.tensor_tensor(h[:, t, NB * c:NB * c + NB], h[:, t, NB * c:NB * c + NB],
                                                ho[:, c, :], ALU.add).then_inc(z_ready, 1)
                rows_T_lo(1 if L == 0 else 4)
                split(25)
                split(26)
                split(27)
                dve.wait_ge(w_used, base + 26)
                for t in range(NT):
                    for c in range(2):
                        nc.vector.tensor_tensor(x[:, t, NB * c:NB * c + NB], x[:, t, NB * c:NB * c + NB],
                                                ps[:, 2 * t + c, :], ALU.add).then_inc(x_done, 1)
                dve.wait_ge(x_done, 4 * L + 4)

            dve.wait_ge(x_landed, 16)
            split_static(0)
            split_static(1)
            mixer(0)

            norm(1)
            rows_T_lo(2)

            def dense_mul(k2, k):
                for t in range(NT):
                    dve.wait_ge(silu_done, k2 + (t + 1))
                    nc.vector.tensor_tensor(ho[:, t, :], ho[:, t, :], ps[:, 2 + t, :], ALU.mult) \
                        .then_inc(act_ready, 1)

            def dense_loT(k):
                dve.wait_ge(aT_hi_done, k)
                nc.vector.tensor_tensor(aT_lo[:], psT, aT_hi[:].bitcast(F32), ALU.subtract).then_inc(aT_lo_done, 1)

            def dense_add(k2, used, c):
                for t in range(NT):
                    if t == 0:
                        dve.wait_ge(y_full, k2 + (c + 1))
                    else:
                        dve.wait_ge(w_used, used)
                    nc.vector.tensor_tensor(x[:, t, NB * c:NB * c + NB], x[:, t, NB * c:NB * c + NB],
                                            ps[:, 6 + t, :], ALU.add).then_inc(y_added, 1)

            for i in range(2, 6):
                split_static(DENSE0 + i)
            dense_mul(0, 0)
            with dve.Fori(0, NSTEP - 1) as n:
                for i in range(2, 6):
                    split_loop(DENSE0 + 4 + i, 6 * n)
                    if i == 2:
                        dense_loT(n + 1)
                dense_mul(2 * n + 2, n)
                dense_add(n * 2, n * 6 + (DENSE0 + 9), 0)
                split_loop(DENSE0 + 4 + 6, 6 * n)
                dense_add(n * 2, n * 6 + (DENSE0 + 10), 1)
                split_loop(DENSE0 + 4 + 7, 6 * n)
                dve.wait_ge(y_added, 4 * n + 4)
            split_static(MIX1)
            dense_loT(NSTEP)
            dense_add(2 * NSTEP - 2, DENSE0 + FF - 1, 0)
            split_static(MIX1 + 1)
            dense_add(2 * NSTEP - 2, DENSE0 + FF, 1)
            dve.wait_ge(y_added, 4 * NSTEP)
            mixer(1)

            norm(3)
            steps = [0]

            def chain(ins):
                steps[0] += 1
                ins.then_inc(route_step, 1)
                dve.wait_ge(route_step, steps[0])

            V = nc.vector
            lg, c1, one1, l2, c2, one2, msk, cmb, rank, tmp = (rt[:, :, i, :] for i in range(10))
            m1, i1, dlt, e21, m2, i2, sm, wa = (r1[:, :, i:i + 1] for i in range(8))
            io8 = iota[:, 0:NE].rearrange("p (a e) -> p a e", a=1).broadcast_to([P, NT, NE])
            wide = lambda a: a.broadcast_to([P, NT, NE])

            dve.wait_ge(logit_full, 1)
            chain(V.tensor_tensor(lg, ps[:, 2:4, 0:NE],
                                  rb[:, :].rearrange("p (a e) -> p a e", a=1).broadcast_to([P, NT, NE]), ALU.add))

            def first_max(src, m, cand, idx, one):
                chain(V.tensor_reduce(m, src, AX_X, ALU.max))
                chain(V.tensor_tensor(cand, src, wide(m), ALU.is_lt))
                chain(V.tensor_scalar(cand, cand, 16.0, None, ALU.mult))
                chain(V.tensor_tensor(cand, cand, io8, ALU.add))
                chain(V.tensor_reduce(idx, cand, AX_X, ALU.min))
                chain(V.tensor_tensor(one, io8, wide(idx), ALU.is_equal))

            first_max(lg, m1, c1, i1, one1)
            chain(V.tensor_scalar(l2, one1, -3.0e38, None, ALU.mult))
            chain(V.tensor_tensor(l2, l2, lg, ALU.add))
            first_max(l2, m2, c2, i2, one2)
            chain(V.tensor_tensor(msk, one1, one2, ALU.add))
            V.tensor_tensor(dlt, m2, m1, ALU.subtract).then_inc(exp_ready, 1)
            V.tensor_copy(tmp, msk).then_inc(mask_ready, 1)
            dve.wait_ge(exp_ready, 2)
            chain(V.tensor_scalar(sm, e21, 1.0, None, ALU.add))
            chain(V.reciprocal(wa, sm))
            chain(V.tensor_tensor(cmb, one2, wide(e21), ALU.mult))
            chain(V.tensor_tensor(cmb, cmb, one1, ALU.add))
            chain(V.tensor_tensor(cmb, cmb, wide(wa), ALU.mult))
            for r in range(2):
                chain(V.tensor_copy(comb[:, :, 1 + NE * r:1 + NE * r + NE], cmb))
            dve.wait_ge(rank_full, 1)
            chain(V.tensor_scalar(rank, ps[:, 2:4, 16:16 + NE], 1000.0, None, ALU.add))
            chain(V.tensor_tensor(rank, rank, msk, ALU.mult))
            chain(V.tensor_scalar(pos[:, :, 0:NE], rank, -1000.0, None, ALU.add))
            chain(V.tensor_scalar(pos[:, :, NE:2 * NE], rank, -1000.0 - P, None, ALU.add))
            chain(V.memset(pos[:, :, 2 * NE:2 * NE + 1], -1.0))
            chain(V.tensor_reduce(njobs_f[:, 0:1], ps[:, 2, 32:32 + NE], AX_X, ALU.max))
            chain(V.tensor_scalar(njobs_f[:, 1:2], njobs_f[:, 0:1], P + 0.5, float(NE), ALU.is_gt, ALU.mult))
            chain(V.tensor_scalar(njobs_f[:, 2:3], njobs_f[:, 1:2], float(NE), None, ALU.add))
            V.tensor_copy(njobs_i[:], njobs_f[:, 2:3]).then_inc(njobs_ready, 1)
            dve.wait_ge(njobs_ready, 1)
            n_jobs = dve.value_load(njobs_i[0:1, 0:1], min_val=NE, max_val=2 * NE)

            def build_sel(col):
                for t in range(NT):
                    V.tensor_scalar(sel[:, t, :], iota[:, :], col(pos, t), None, ALU.is_equal).then_inc(sel_ready, 1)

            def gather_lo(k):
                dve.wait_ge(g_hi, k)
                V.tensor_tensor(hT_lo[:, 0:D], ps23, hT_hi[:, 0:D].bitcast(F32), ALU.subtract).then_inc(g_lo, 1)

            def scatter_add(k4, col):
                for t in range(NT):
                    for c in range(2):
                        i = 2 * t + c
                        dve.wait_ge(scat_full, k4 + (i + 1))
                        V.scalar_tensor_tensor(x[:, t, NB * c:NB * c + NB], ps[:, 2 + c, :], col(comb, t),
                                               x[:, t, NB * c:NB * c + NB], ALU.mult, ALU.add) \
                            .then_inc(scat_added, 1)

            V.memset(os_hi[:].bitcast(F32), 0.0).then_inc(init_done, 1)
            V.memset(os_lo[:].bitcast(F32), 0.0).then_inc(init_done, 1)
            dve.wait_ge(init_done, 5)
            build_sel(lambda a, t: a[:, t, 0:1])
            gather_lo(1)
            with dve.Fori(0, n_jobs) as j:
                u42, u7, u4 = dve.snap(j * FF), dve.snap(j * NSTEP), dve.snap(j * 4)

                def split(i):
                    split_loop(MOE0 + i, u42)

                def mul(n):
                    dve.wait_ge(silu_done, u7 + (2 * NSTEP + n + 1))
                    V.tensor_tensor(ho[:, 0, :], ho[:, 0, :], ps[:, 1, :], ALU.mult).then_inc(act_ready, 1)

                def loT(n):
                    dve.wait_ge(aT_hi_done, u7 + (NSTEP + n + 1))
                    V.tensor_tensor(aT_lo[:, 0:NB], ps[:, 4, :], aT_hi[:, 0:NB].bitcast(F32), ALU.subtract) \
                        .then_inc(aT_lo_done, 1)

                for i in range(2, 6):
                    split(i)
                mul(0)
                scatter_add(u4, lambda a, t: a[:, t, bass.ds(j, 1)])
                for n in range(1, NSTEP):
                    s = 6 * n - 2
                    split(s + 2)
                    loT(n - 1)
                    split(s + 3)
                    split(s + 4)
                    split(s + 5)
                    mul(n)
                    if n == 3:
                        dve.wait_ge(selT_full, j + 1)
                        build_sel(lambda a, t: a[:, t, bass.ds(j + 1, 1)])
                    split(s + 6)
                    split(s + 7)
                loT(NSTEP - 1)
                gather_lo(j + 2)
                with dve.If(j + 1 < n_jobs):
                    split(FF)
                    split(FF + 1)
                dve.wait_ge(yj_hi, j + 1)
                V.tensor_tensor(os_lo[:], psY, os_hi[:].bitcast(F32), ALU.subtract).then_inc(yj_lo, 1)
                dve.wait_ge(scat_added, u4 + 4)
            scatter_add(dve.snap(n_jobs * 4), lambda a, t: a[:, t, bass.ds(n_jobs, 1)])
            dve.wait_ge(scat_added, n_jobs * 4 + 4)
            norm(4)

        @block.tensor
        def _(pe):
            mm = nc.tensor.matmul

            def three(dst, a_hi, a_lo, b_hi, b_lo, start, stop):
                mm(dst, a_hi, b_hi, start=start, stop=False)
                mm(dst, a_lo, b_hi, start=False, stop=False)
                return mm(dst, a_hi, b_lo, start=False, stop=stop)

            def rows_T(K, src, ready):
                for r in range(4):
                    t, c = divmod(r, 2)
                    if c == 0:
                        ready(t)
                    if r >= 2:
                        pe.wait_ge(hT_lo_done, 4 * K + r - 1)
                    for k in range(4):
                        last = nc.tensor.transpose(ps[:, 4 + r % 2, P * k:P * k + P],
                                                   src[:, t, P * (4 * c + k):P * (4 * c + k) + P], ident[:])
                    last.then_inc(hT_full, 1)

            def mixer(L):
                base = 0 if L == 0 else MIX1

                def proj_block(m, n):
                    b = base + m
                    chunks = 8 if m == 10 else 4
                    cols = 256 if m == 10 else NB
                    first = m == 10 or (m % 2 == 0 if m < 10 else m % 2 == 1)
                    last_half = m == 10 or not first
                    k0 = 0 if first else 4
                    pe.wait_ge(lo_ready, b + 1)
                    hi, lo = wblock(whi, b, SPL, chunks), wblock(wlo, b, SPL, chunks)
                    for t in range(NT):
                        q = 2 * n + t
                        if first and q >= 4:
                            pe.wait_ge(proj_evac, NPROD * L + (q - 3 if q < 12 else q - 1))
                        for k in range(chunks):
                            a = SEQ * (k0 + k) + P * t
                            ins = three(ps[:, proj_bank(q), 0:cols], hT_hi[:, a:a + P], hT_lo[:, a:a + P],
                                        hi[:, k, :], lo[:, k, :], first and k == 0, last_half and k == chunks - 1)
                    ins.then_inc(w_used, 1)

                def fourier_a():
                    pe.wait_ge(proj_evac, NPROD * L + 2)
                    pe.wait_ge(dft_landed, 16 * L + 16)
                    for g in range(FG):
                        if g >= 2:
                            pe.wait_ge(fa_evac, FG * L + g - 1)
                        for t in range(NT):
                            ins = mm(ps[:, 6 + g % 2, :], ho[:, t, P * g:P * g + P], dftpos[:, t, :],
                                     start=t == 0, stop=t == NT - 1)
                        ins.then_inc(fa_full, 1)

                def fourier_b():
                    for i in range(2):
                        pe.wait_ge(fa_evac, FG * L + 4)
                        for g in (2 * i, 2 * i + 1):
                            dst = ps[:, 6 + i, SEQ * (g % 2):SEQ * (g % 2) + SEQ]
                            mm(dst, dftch[:, 0, :], fab[:, g, 0:SEQ], start=True, stop=False)
                            ins = mm(dst, dftch[:, 1, :], fab[:, g, SEQ:2 * SEQ], start=False, stop=True)
                        ins.then_inc(fb_full, 1)

                def qk_T(i):
                    part, t = divmod(i, 2)
                    pe.wait_ge(rope_done, 4 * L + i + 1)
                    if i:
                        pe.wait_ge(qkT_evac, 4 * L + i)
                    for c in range(6):
                        a = AW * part + P * c
                        ins = nc.tensor.transpose(psT[:, P * c:P * c + P], qg[:, t, a:a + P], ident[:])
                    ins.then_inc(qkT_full, 1)

                def groups(t):
                    return (0, 1, 2) if t == 0 else (1, 2, 0)

                def scores(u):
                    t, j = divmod(u, HG)
                    if u == 0:
                        pe.wait_ge(qkT_evac, 4 * L + 4)
                        pe.wait_ge(fb_lo, 2 * L + 2)
                    else:
                        pe.wait_ge(sc_used, 8 * L + u)
                    for i, g in enumerate(groups(t)):
                        head = HG * g + j
                        c, p0 = head // 2, HD * (head % 2)
                        ins = mm(psY[:, SEQ * i:SEQ * i + SEQ], qkTc[p0:p0 + HD, c, P * t:P * t + P],
                                 qkTc[p0:p0 + HD, 6 + c, :], start=True, stop=True)
                    ins.then_inc(sc_full, 1)

                def prob_T(u):
                    pe.wait_ge(p_ready, 8 * L + u + 1)
                    if 8 * L + u >= 1:
                        pe.wait_ge(pT_evac_a, 8 * L + u)
                        pe.wait_ge(pT_evac_d, 8 * L + u)
                    for c in range(6):
                        ins = nc.tensor.transpose(psT[:, P * c:P * c + P], p_sb[:, P * c:P * c + P], ident[:])
                    ins.then_inc(pT_full, 1)

                def prob_v(u):
                    t, j = divmod(u, HG)
                    pe.wait_ge(pT_evac_a, 8 * L + u + 1)
                    pe.wait_ge(pT_evac_d, 8 * L + u + 1)
                    if u < 2:
                        pe.wait_ge(proj_evac, NPROD * L + 11 + u)
                    elif u < 6:
                        pe.wait_ge(o_done, 8 * L + u - 1)
                    for c in range(6):
                        head = HG * groups(t)[c // 2] + j
                        ins = mm(pv_out(u), pT[:, P * c:P * c + P],
                                 v[:, c % 2, HD * head:HD * head + HD], start=c == 0, stop=c == 5)
                    ins.then_inc(pv_full, 1)

                N = 2 * L
                rows_T(0 if L == 0 else 3, h, lambda t: pe.wait_ge(h_ready, 2 * N + t + 1))
                pe.wait_ge(hT_lo_done, 4 * (0 if L == 0 else 3) + 4)
                for m in range(11):
                    if m >= 8:
                        qk_T(m - 8)
                    proj_block(m, m // 2)
                    if m == 5:
                        fourier_a()
                    if m == 7:
                        fourier_b()
                qk_T(3)
                for i in range(10):
                    if i < 8:
                        scores(i)
                    if 1 <= i <= 8:
                        prob_T(i - 1)
                    if i >= 2:
                        prob_v(i - 2)
                    if i < 8:
                        proj_block(11 + i, 6 + i // 2)
                    else:
                        b = base + 11 + i
                        if i == 8:
                            pe.wait_ge(proj_evac, NPROD * L + 20)
                            pe.wait_ge(o_done, 8 * L + 6)
                        pe.wait_ge(lo_ready, b + 1)
                        hi, lo = wblock(whi, b, SPL, 2), wblock(wlo, b, SPL, 2)
                        for t in range(NT):
                            for c in range(2):
                                for k in range(2):
                                    a = SEQ * (2 * (i - 8) + k) + P * t
                                    ins = three(ps[:, 2 * t + c, :], aT_hi[:, a:a + P], aT_lo[:, a:a + P],
                                                hi[:, k, NB * c:NB * c + NB], lo[:, k, NB * c:NB * c + NB],
                                                i == 8 and k == 0, i == 9 and k == 1)
                        ins.then_inc(w_used, 1)
                pe.wait_ge(o_done, 8 * L + 8)
                for c in range(2):
                    for t in range(NT):
                        ins = nc.tensor.transpose(ps[:, 4, SEQ * c + P * t:SEQ * c + P * t + P],
                                                  o[:, t, P * c:P * c + P], ident[:])
                ins.then_inc(oT_full, 1)
                b = base + 21
                pe.wait_ge(oT_lo, L + 1)
                pe.wait_ge(lo_ready, b + 1)
                hi, lo = wblock(whi, b, SPL, 2), wblock(wlo, b, SPL, 2)
                for t in range(NT):
                    for c in range(2):
                        for k in range(2):
                            a = SEQ * k + P * t
                            ins = three(ps[:, 4 + 2 * t + c, :], os_hi[:, a:a + P], os_lo[:, a:a + P],
                                        hi[:, k, NB * c:NB * c + NB], lo[:, k, NB * c:NB * c + NB], k == 0, k == 1)
                ins.then_inc(w_used, 1)
                K = 1 if L == 0 else 4
                rows_T(K, h, lambda t: pe.wait_ge(z_ready, 4 * L + 2 * t + 2))
                pe.wait_ge(hT_lo_done, 4 * K + 4)
                for i in range(4):
                    b = base + 22 + i
                    pe.wait_ge(lo_ready, b + 1)
                    hi, lo = wblock(whi, b, SPL, 2), wblock(wlo, b, SPL, 2)
                    for t in range(NT):
                        for c in range(2):
                            for k in range(2):
                                a = SEQ * (2 * i + k) + P * t
                                ins = three(ps[:, 2 * t + c, :], hT_hi[:, a:a + P], hT_lo[:, a:a + P],
                                            hi[:, k, NB * c:NB * c + NB], lo[:, k, NB * c:NB * c + NB],
                                            i == 0 and k == 0, i == 3 and k == 1)
                    ins.then_inc(w_used, 1)

            pe.wait_ge(const_landed, 16 * 8)
            mixer(0)

            rows_T(2, h, lambda t: pe.wait_ge(h_ready, 2 + t + 1))
            pe.wait_ge(hT_lo_done, 12)

            def dense_up(s, add):
                for i in range(4):
                    pe.wait_ge(lo_ready, add + (s + i + 1))
                    hi, lo = wblock(whi, s + i, SPL, 4), wblock(wlo, s + i, SPL, 4)
                    for t in range(NT):
                        for k in range(4):
                            a = SEQ * (4 * (i % 2) + k) + P * t
                            ins = three(ps[:, 2 * (i // 2) + t, :], hT_hi[:, a:a + P], hT_lo[:, a:a + P],
                                        hi[:, k, :], lo[:, k, :], i % 2 == 0 and k == 0, i % 2 == 1 and k == 3)
                    ins.then_inc(w_used, 1)

            def dense_down(s, add, steps, added):
                pe.wait_ge(aT_lo_done, steps)
                for c in range(2):
                    pe.wait_ge(lo_ready, add + (s + c + 1))
                    hi, lo = wblock(whi, s + c, SPL, 4), wblock(wlo, s + c, SPL, 4)
                    for t in range(NT):
                        if c == 1:
                            pe.wait_ge(y_added, added + (t + 1))
                        for k in range(4):
                            a = NB * t + P * k
                            ins = three(ps[:, 6 + t, :], aT_hi[:, a:a + P], aT_lo[:, a:a + P],
                                        hi[:, k, :], lo[:, k, :], k == 0, k == 3)
                        ins.then_inc(y_full if t == 0 else w_used, 1)

            def dense_T(ready):
                pe.wait_ge(act_ready, ready)
                for t in range(NT):
                    for k in range(4):
                        ins = nc.tensor.transpose(ps[:, 4 + t, P * k:P * k + P], ho[:, t, P * k:P * k + P], ident[:])
                ins.then_inc(aT_full, 1)

            dense_up(DENSE0, 0)
            dense_T(2)
            with pe.Fori(0, NSTEP - 1) as n:
                n6, n4 = pe.snap(n * 6), pe.snap(n * 4)
                dense_up(DENSE0 + 4, n6)
                with pe.If(n > 0):
                    pe.wait_ge(y_added, n4)
                dense_down(DENSE0 + 8, n6, n + 1, n4)
                dense_T(2 * n + 4)
            pe.wait_ge(y_added, 4 * NSTEP - 4)
            dense_down(DENSE0 + FF - 2, 0, NSTEP, 4 * NSTEP - 4)
            mixer(1)

            for r in range(4):
                t, c = divmod(r, 2)
                pe.wait_ge(h_ready, 6 + t + 1)
                if r >= 2:
                    pe.wait_ge(rT_evac, r - 1)
                for k in range(4):
                    ins = nc.tensor.transpose(ps[:, 4 + r % 2, P * k:P * k + P],
                                              h[:, t, P * (4 * c + k):P * (4 * c + k) + P], ident[:])
                ins.then_inc(rT_full, 1)
            pe.wait_ge(rT_evac, 4)
            for t in range(NT):
                for k in range(KD):
                    ins = mm(ps[:, 2 + t, 0:NE], routT[:, k, P * t:P * t + P], rw[:, k, :],
                             start=k == 0, stop=k == KD - 1)
            ins.then_inc(logit_full, 1)
            pe.wait_ge(init_done, 3)
            pe.wait_ge(mask_ready, 1)
            msk = [rt[:, t, 9, :] for t in range(NT)]
            mm(ps[:, 2, 16:16 + NE], before[:], msk[0], start=True, stop=True)
            mm(ps[:, 3, 16:16 + NE], ones[:], msk[0], start=True, stop=False)
            mm(ps[:, 3, 16:16 + NE], before[:], msk[1], start=False, stop=True)
            mm(ps[:, 2, 32:32 + NE], ones[:], msk[0], start=True, stop=False)
            mm(ps[:, 2, 32:32 + NE], ones[:], msk[1], start=False, stop=True).then_inc(rank_full, 1)
            pe.wait_ge(njobs_ready, 1)
            n_jobs = pe.value_load(njobs_i[0:1, 0:1], min_val=NE, max_val=2 * NE)

            def gather(sel_count):
                pe.wait_ge(sel_ready, sel_count)
                for k in range(KD):
                    for t in range(NT):
                        ins = mm(ps23[:, P * k:P * k + P], h[:, t, P * k:P * k + P], sel[:, t, :],
                                 start=t == 0, stop=t == NT - 1)
                ins.then_inc(g_full, 1)

            def scatter(added):
                for t in range(NT):
                    for c in range(2):
                        if t == 1:
                            pe.wait_ge(scat_added, added + (c + 1))
                        lhs = selT[:, P * t:P * t + P]
                        mm(ps[:, 2 + c, :], lhs, os_hi[:, NB * c:NB * c + NB], start=True, stop=False)
                        ins = mm(ps[:, 2 + c, :], lhs, os_lo[:, NB * c:NB * c + NB], start=False, stop=True)
                        ins.then_inc(scat_full, 1)

            gather(2)
            pe.wait_ge(init_done, 5)
            with pe.Fori(0, n_jobs) as j:
                u42, u7, u4 = pe.snap(j * FF), pe.snap(j * NSTEP), pe.snap(j * 4)

                def up(s):
                    for i in range(4):
                        b = MOE0 + s + i
                        pe.wait_ge(lo_ready, u42 + (b + 1))
                        hi, lo = wblock(whi, b, SPL, 4), wblock(wlo, b, SPL, 4)
                        for k in range(4):
                            a = P * (4 * (i % 2) + k)
                            ins = three(ps[:, i // 2, :], hT_hi[:, a:a + P], hT_lo[:, a:a + P],
                                        hi[:, k, :], lo[:, k, :], i % 2 == 0 and k == 0, i % 2 == 1 and k == 3)
                        ins.then_inc(w_used, 1)

                def hidden_T(n):
                    pe.wait_ge(act_ready, u7 + (2 * NSTEP + n + 1))
                    for k in range(4):
                        ins = nc.tensor.transpose(ps[:, 4, P * k:P * k + P], ho[:, 0, P * k:P * k + P], ident[:])
                    ins.then_inc(aT_full, 1)

                def down(n, s):
                    pe.wait_ge(aT_lo_done, u7 + (NSTEP + n + 1))
                    for c in range(2):
                        b = MOE0 + s + c
                        pe.wait_ge(lo_ready, u42 + (b + 1))
                        hi, lo = wblock(whi, b, SPL, 4), wblock(wlo, b, SPL, 4)
                        for k in range(4):
                            ins = three(ps[:, 6 + c, :], aT_hi[:, P * k:P * k + P], aT_lo[:, P * k:P * k + P],
                                        hi[:, k, :], lo[:, k, :], n == 0 and k == 0, n == NSTEP - 1 and k == 3)
                        ins.then_inc(w_used, 1)

                pe.wait_ge(g_lo, j + 1)
                up(0)
                with pe.If(j > 0):
                    pe.wait_ge(yj_lo, j)
                scatter(u4)
                hidden_T(0)
                for n in range(1, NSTEP):
                    s = 6 * n - 2
                    up(s)
                    if n == 1:
                        for t in range(NT):
                            ins = nc.tensor.transpose(ps[:, 5, P * t:P * t + P], sel[:, t, :], ident[:])
                        ins.then_inc(selT_full, 1)
                    down(n - 1, s + 4)
                    hidden_T(n)
                pe.wait_ge(scat_added, u4 + 4)
                gather(2 * j + 4)
                down(NSTEP - 1, FF - 2)
            pe.wait_ge(yj_lo, n_jobs)
            scatter(pe.snap(n_jobs * 4))


def _constants():
    import numpy as np
    f = np.float32
    s = np.arange(SEQ, dtype=np.float64)
    ang = 2 * np.pi * np.outer(s, s) / SEQ
    pos = np.concatenate([np.cos(ang), np.sin(ang)], 1) / np.sqrt(SEQ)
    c = np.arange(P, dtype=np.float64)
    angc = 2 * np.pi * np.outer(c, c) / P
    ch = np.stack([np.cos(angc), -np.sin(angc)], 1) / np.sqrt(P)
    q = np.arange(P)[:, None]
    k = np.arange(SEQ)[None, :]
    no = f(-1e30)
    band = [np.where(np.abs(q + P * t - k) <= HD, f(0), no) for t in range(NT)]
    dil = [np.where((q - k) % d == 0, f(0), no) for d in (4, 16)]
    mask = np.concatenate([band[0], dil[0], dil[1], band[1]], 1).astype(f)
    half = HD // 2
    inv = f(10000.0) ** (-np.arange(half, dtype=f) * f(2.0) / f(HD))
    a = (np.arange(SEQ, dtype=f)[:, None] * inv[None, :].astype(f)).astype(f)
    co, si = np.cos(a), np.sin(a)
    rope = np.stack([np.concatenate([co, co], 1), np.concatenate([-si, si], 1)], 1)
    rope = rope.reshape(NT, P, 2, HD).transpose(1, 0, 2, 3)
    return {
        "c_ident": np.eye(P, dtype=f),
        "c_dftpos": pos.reshape(NT, P, NB).transpose(1, 0, 2).astype(f),
        "c_dftch": ch.astype(f),
        "c_mask": mask,
        "c_rope": rope.astype(f),
        "c_iota": np.tile(np.arange(P, dtype=f), (P, 1)),
        "c_before": np.triu(np.ones((P, P), f), 1),
    }


_INS = ["x", "ln_mix", "w_in", "w_fourier", "w_attn", "w_out", "ln_ffn", "dense_w1", "dense_w3", "dense_w2",
        "router_w", "router_b", "moe_w1", "moe_w3", "moe_w2", "ln_final"]


def kernel(**inputs):
    import numpy as np
    import concourse.bacc as bacc
    from concourse.bass_utils import run_bass_kernel_spmd

    nc = bacc.Bacc("TRN2", target_bir_lowering=False, num_devices=1)
    arrays, args = {}, []
    feeds = {name: np.asarray(inputs[name]) for name in _INS}
    feeds.update(_constants())
    for name, a in feeds.items():
        a = np.ascontiguousarray(a)
        arrays[f"in_{name}"] = a
        args.append(nc.dram_tensor(f"in_{name}", a.shape, mybir.dt.from_np(a.dtype), kind="ExternalInput").ap())
    args.append(nc.dram_tensor("out_0", (1, SEQ, D), F32, kind="ExternalOutput").ap())
    build(nc, *args)
    r = run_bass_kernel_spmd(nc, [arrays], core_ids=[0])
    return r.results[0]["out_0"]
```

```python
from contextlib import ExitStack

import concourse.bass as bass
from concourse import mybir

F32 = mybir.dt.float32
F32R = mybir.dt.float32r
I32 = mybir.dt.int32
ALU = mybir.AluOpType
ACT = mybir.ActivationFunctionType
AX_X = mybir.AxisListType.X

P = 128
D = 1024
SEQ = 256
NT = SEQ // P
KD = D // P
NB = 512
FG = 4
HG = 4
HD = 64
NG = 3
AW = NG * HG * HD
FFN = 3584
NSTEP = FFN // NB
NE = 8
RAW = 6
SPL = 3
BLK = 2048
MIX = 26
FF = 6 * NSTEP
DENSE0 = MIX
MIX1 = MIX + FF
MOE0 = 2 * MIX + FF
EPS = 1e-6
QS = HD ** -0.5
NPROD = 20
RES = 4
HALF = SEQ // RES
KEYS = SEQ + 2 * P


def build(nc, x_in, ln_mix, w_in, w_fourier, w_attn, w_out, ln_ffn, dense_w1, dense_w3, dense_w2,
          router_w, router_b, moe_w1, moe_w3, moe_w2, ln_final,
          c_ident, c_dftpos, c_dftch, c_mask, c_rope, c_iota, c_before, out):
    with ExitStack() as ctx:
        def sb(name, shape, dt=F32):
            return ctx.enter_context(nc.sbuf_tensor(name, shape, dt))

        def sem(name):
            return ctx.enter_context(nc.semaphore(name))

        raw = sb("raw", [P, RAW, BLK])
        whi = sb("whi", [P, SPL, BLK], F32R)
        wlo = sb("wlo", [P, SPL, BLK], F32R)
        x = sb("x", [P, NT, D])
        h = sb("h", [P, NT, D])
        hT_hi = sb("hT_hi", [P, KD * SEQ], F32R)
        hT_lo = sb("hT_lo", [P, KD * SEQ], F32R)
        aT_hi = sb("aT_hi", [P, NT * NB], F32R)
        aT_lo = sb("aT_lo", [P, NT * NB], F32R)
        ho = sb("ho", [P, NT, NB])
        qg = sb("qg", [P, NT, 2 * D])
        v = sb("v", [P, NT, AW])
        qkT = sb("qkT", [P, 3072])
        att = sb("att", [P, 6 * KEYS])
        os_hi = sb("os_hi", [P, D], F32R)
        os_lo = sb("os_lo", [P, D], F32R)
        ident = sb("ident", [P, P])
        dftch = sb("dftch", [P, 2, P])
        mask = sb("mask", [P, 2 * SEQ + 2 * P])
        rope = sb("rope", [P, NT, 2, HD])
        iota = sb("iota", [P, P + NE])
        before = sb("before", [P, P])
        rw = sb("rw", [P, KD, NE])
        rb = sb("rb", [P, NE])
        sel = sb("sel", [P, NT, P])
        selT = sb("selT", [P, SEQ], F32R)
        ssq = sb("ssq", [P, 5 * NT])
        std = sb("std", [P, 5 * NT])
        rstd = sb("rstd", [P, 5 * NT])
        eps = sb("eps", [P, 1])
        warm = sb("warm", [P, 8])
        mx = sb("mx", [P, 2])
        nmx = sb("nmx", [P, 2])
        den = sb("den", [P, 16])
        rden = sb("rden", [P, 16])
        njobs_f = sb("njobs_f", [P, 4])
        njobs_i = sb("njobs_i", [P, 1], I32)

        ps = ctx.enter_context(nc.psum_tensor("ps", [P, 8, NB], F32))

        gain = att[:, 0:D]
        fab = att[:, 0:FG * NB].rearrange("p (g c) -> p g c", g=FG)
        s_sb, p_sb, pT = ([att[:, KEYS * (2 * i + b):KEYS * (2 * i + b) + KEYS] for b in range(2)] for i in range(3))
        o = h[:, 0, 0:NT * HG * HD].rearrange("p (t c) -> p t c", t=NT)
        dftpos = qkT[:, 0:NT * NB].rearrange("p (t c) -> p t c", t=NT)
        qkTc = qkT[:, :].rearrange("p (c s) -> p c s", c=12)
        routT = qg[:, :, :].rearrange("p a b -> p (a b)")[:, 0:KD * SEQ].rearrange("p (k s) -> p k s", k=KD)
        Y0 = 6
        psY = ps[:, 6:8, :].rearrange("p b c -> p (b c)")
        psT = ps[:, 4:6, :].rearrange("p b c -> p (b c)")
        ps23 = ps[:, 2:4, :].rearrange("p b c -> p (b c)")

        v_end = v[:, :, :].rearrange("p t c -> p (t c)")
        rt = v_end[:, 0:8 * NT * NE].rearrange("p (t i e) -> p t i e", t=NT, i=8)
        r1 = v_end[:, 128:128 + 8 * NT].rearrange("p (t i) -> p t i", t=NT)
        JC = 2 * NE + 1
        comb = v_end[:, 144:144 + NT * JC].rearrange("p (t j) -> p t j", t=NT)
        pos = v_end[:, 192:192 + NT * JC].rearrange("p (t j) -> p t j", t=NT)
        ones = v_end[:, 256:256 + P]

        x_landed = [sem(f"x_landed{t}") for t in range(NT)]
        ident_landed = sem("ident_landed")
        const_landed = sem("const_landed")
        gain_landed = sem("gain_landed")
        dft_landed = sem("dft_landed")
        raw_landed = [sem(f"raw_landed{i}") for i in range(RAW)]
        hi_ready = sem("hi_ready")
        lo_ready = sem("lo_ready")
        w_used = sem("w_used")
        init_done = sem("init_done")
        ssq_ready = sem("ssq_ready")
        std_ready = sem("std_ready")
        rstd_ready = sem("rstd_ready")
        warm_done = sem("warm_done")
        h_ready = sem("h_ready")
        hT_full = sem("hT_full")
        hT_hi_done = sem("hT_hi_done")
        hT_lo_done = sem("hT_lo_done")
        proj_evac = sem("proj_evac")
        rope_step = sem("rope_step")
        rope_done = sem("rope_done")
        qkT_full = sem("qkT_full")
        qkT_evac = sem("qkT_evac")
        fa_full = sem("fa_full")
        fa_evac = sem("fa_evac")
        fb_full = sem("fb_full")
        fb_hi = sem("fb_hi")
        fb_lo = sem("fb_lo")
        sc_full = sem("sc_full")
        sc_used = sem("sc_used")
        nmx_ready = sem("nmx_ready")
        p_ready = sem("p_ready")
        pT_full = sem("pT_full")
        pT_evac = sem("pT_evac")
        pv_full = sem("pv_full")
        rden_ready = sem("rden_ready")
        o_done = sem("o_done")
        oT_full = sem("oT_full")
        oT_hi = sem("oT_hi")
        oT_lo = sem("oT_lo")
        ya_half = sem("ya_half")
        xo_half = sem("xo_half")
        zf_done = sem("zf_done")
        za_done = sem("za_done")
        z_ready = sem("z_ready")
        x_done = sem("x_done")
        silu_done = sem("silu_done")
        act_ready = sem("act_ready")
        aT_full = sem("aT_full")
        aT_hi_done = sem("aT_hi_done")
        aT_lo_done = sem("aT_lo_done")
        y_full = sem("y_full")
        y_added = sem("y_added")
        rT_full = sem("rT_full")
        rT_evac = sem("rT_evac")
        logit_full = sem("logit_full")
        exp_ready = sem("exp_ready")
        route_step = sem("route_step")
        mask_ready = sem("mask_ready")
        rank_full = sem("rank_full")
        count_max = sem("count_max")
        njobs_ready = sem("njobs_ready")
        sel_ready = sem("sel_ready")
        g_full = sem("g_full")
        g_hi = sem("g_hi")
        g_lo = sem("g_lo")
        yj_hi = sem("yj_hi")
        yj_lo = sem("yj_lo")
        selT_full = sem("selT_full")
        selT_ready = sem("selT_ready")
        scat_full = sem("scat_full")
        scat_added = sem("scat_added")
        out_done = sem("out_done")

        def proj_bank(q):
            return q % 4 if q < 12 else q % 2

        def pv_out(u):
            return ps[:, 2 + u % 2 if u < 6 else u, 0:HD]

        def by_residue(rows):
            return rows[0].rearrange("(i r) d -> r i d", r=RES)

        def k_rows(w):
            return w.rearrange("(k p) n -> p k n", p=P)

        def mix_src(L, m):
            wi = k_rows(w_in[L])
            if m < 10:
                return wi[:, 4 * (m % 2):4 * (m % 2) + 4, NB * (m // 2):NB * (m // 2) + NB], 4
            if m == 10:
                return wi[:, :, 2560:2816], 8
            if m < 19:
                a = 2816 + NB * ((m - 11) // 2)
                half = (m - 11) % 2
                return wi[:, 4 * half:4 * half + 4, a:a + NB], 4
            if m < 21:
                return k_rows(w_fourier[L])[:, 2 * (m - 19):2 * (m - 19) + 2, :], 2
            if m == 21:
                return k_rows(w_attn[L]), 2
            return k_rows(w_out[L])[:, 2 * (m - 22):2 * (m - 22) + 2, :], 2

        def wblock(buf, b_static, n, chunks):
            return buf[:, b_static % n, :].rearrange("p (k c) -> p k c", k=chunks)

        block = ctx.enter_context(nc.Block())

        @block.sync
        def _(sp):
            def load(b, b_static, src, chunks, first=False):
                if not first:
                    sp.wait_ge(lo_ready, b - RAW + 1)
                sp.dma_start(wblock(raw, b_static, RAW, chunks), src).then_inc(raw_landed[b_static % RAW], 16)

            def load_gain(src):
                sp.dma_start(gain, src.partition_broadcast(P)).then_inc(gain_landed, 16)

            for t in range(NT):
                for r in range(2):
                    sp.dma_start(x[HALF * r:HALF * r + HALF, t, :], by_residue(x_in)[2 * t + r]) \
                        .then_inc(x_landed[t], 16)
            load_gain(ln_mix[0])
            for L in range(2):
                base = 0 if L == 0 else MIX1
                if L == 1:
                    sp.wait_ge(h_ready, 8)
                    load_gain(ln_mix[1])
                for m in range(MIX):
                    if m == 4:
                        if L == 1:
                            sp.wait_ge(pv_full, 8)
                        sp.dma_start(dftpos, c_dftpos).then_inc(dft_landed, 16)
                    src, chunks = mix_src(L, m)
                    load(base + m, base + m, src, chunks, first=base + m < RAW)
                sp.wait_ge(pv_full, 8 * L + 8)
                load_gain(ln_ffn[L])
                if L == 0:
                    w1, w3, w2 = k_rows(dense_w1[0]), k_rows(dense_w3[0]), k_rows(dense_w2[0])
                    for i in range(4):
                        w = w1 if i < 2 else w3
                        load(DENSE0 + i, DENSE0 + i, w[:, 4 * (i % 2):4 * (i % 2) + 4, 0:NB], 4)
                    with sp.Fori(1, NSTEP) as n:
                        for i in range(6):
                            s = DENSE0 + 4 + i
                            if i < 4:
                                w = w1 if i < 2 else w3
                                src = w[:, 4 * (i % 2):4 * (i % 2) + 4, bass.ds(n * NB, NB)]
                            else:
                                src = w2[:, bass.ds(4 * n - 4, 4), NB * (i - 4):NB * (i - 4) + NB]
                            load(DENSE0 - 2 + 6 * n + i, s, src, 4)
                    for i in range(2):
                        b = DENSE0 + 6 * NSTEP - 2 + i
                        load(b, b, w2[:, 4 * NSTEP - 4:4 * NSTEP, NB * i:NB * i + NB], 4)

            def load_expert(job, e):
                w1 = moe_w1[0][bass.ds(e, 1)].rearrange("e (k p) n -> p (e k) n", p=P)
                w3 = moe_w3[0][bass.ds(e, 1)].rearrange("e (k p) n -> p (e k) n", p=P)
                w2 = moe_w2[0][bass.ds(e, 1)].rearrange("e (k p) n -> p (e k) n", p=P)
                for i in range(FF):
                    n, q = divmod(i + 2, 6)
                    if i < 4:
                        n, q = 0, i
                    if i >= FF - 2:
                        n, q = NSTEP, 4 + i - (FF - 2)
                    if q < 4:
                        w = w1 if q < 2 else w3
                        src = w[:, 4 * (q % 2):4 * (q % 2) + 4, NB * n:NB * n + NB]
                    else:
                        src = w2[:, 4 * n - 4:4 * n, NB * (q - 4):NB * (q - 4) + NB]
                    load(FF * job + (MOE0 + i), MOE0 + i, src, 4)

            with sp.Fori(0, NE) as e:
                load_expert(e, e)
            sp.wait_ge(njobs_ready, 1)
            n_jobs = sp.value_load(njobs_i[0:1, 0:1], min_val=NE, max_val=2 * NE)
            with sp.If(n_jobs > NE):
                with sp.Fori(0, NE) as e2:
                    load_expert(e2 + NE, e2)
            sp.wait_ge(h_ready, 16)
            load_gain(ln_final)
            for t in range(NT):
                sp.wait_ge(h_ready, 18 + 2 * t)
                for r in range(2):
                    sp.dma_start(by_residue(out)[2 * t + r], h[HALF * r:HALF * r + HALF, t, :]).then_inc(out_done, 16)
            sp.wait_ge(out_done, 64)

        @block.scalar
        def _(act):
            def split_loop(s, landed_add, used_add):
                act.wait_ge(raw_landed[s % RAW], landed_add + (16 * (s // RAW) + 16))
                act.wait_ge(w_used, used_add + (s - SPL + 1))
                nc.scalar.copy(whi[:, s % SPL, :], raw[:, s % RAW, :]).then_inc(hi_ready, 1)

            def norm_std(N, x_complete):
                act.wait_ge(init_done, 1)
                nc.scalar.activation(warm[:, N:N + 1], eps[:], ACT.Sqrt).then_inc(warm_done, 1)
                for t in range(NT):
                    x_complete(t)
                    i = 2 * N + t
                    nc.scalar.activation(h[:, t, :], x[:, t, :], ACT.Square, accum_out=ssq[:, i:i + 1]) \
                        .then_inc(ssq_ready, 1)
                    act.wait_ge(ssq_ready, i + 1)
                    nc.scalar.activation(std[:, i:i + 1], ssq[:, i:i + 1], ACT.Sqrt, bias=eps[:], scale=1.0 / D) \
                        .then_inc(std_ready, 1)

            def rows_T_hi(K, places=range(4), by_half=False):
                for r in places:
                    t, c = (r % 2, r // 2) if by_half else (r // 2, r % 2)
                    act.wait_ge(hT_full, 4 * K + r + 1)
                    dst = hT_hi[:, :].rearrange("p (k s) -> p k s", k=KD)[:, 4 * c:4 * c + 4, P * t:P * t + P]
                    nc.scalar.copy(dst, ps[:, 4 + r % 2, :].rearrange("p (k s) -> p k s", k=4)) \
                        .then_inc(hT_hi_done, 1)

            act.dma_start(ident[:], c_ident).then_inc(ident_landed, 16)
            late_consts = ((dftch[:], c_dftch), (mask[:], c_mask), (rope[:], c_rope),
                           (iota[:], c_iota), (before[:], c_before), (rw[:], k_rows(router_w[0])),
                           (rb[:], router_b[0].partition_broadcast(P)))

            def dense_complete(t):
                act.wait_ge(y_added, 4 * NSTEP - 1 + t)

            def mixer(L):
                base = 0 if L == 0 else MIX1

                def split(m):
                    split_static(base + m)

                def evac(q):
                    n, t = divmod(q, 2)
                    last = 2 * n + 1 if n < 5 else 2 * n
                    act.wait_ge(w_used, base + last + 1)
                    src = ps[:, proj_bank(q), :]
                    if n == 0:
                        nc.scalar.copy(ho[:, t, :], src).then_inc(proj_evac, 1)
                    elif n < 4:
                        nc.scalar.copy(qg[:, t, NB * (n - 1):NB * n], src).then_inc(proj_evac, 1)
                    elif n == 4:
                        nc.scalar.copy(v[:, t, 0:NB], src).then_inc(proj_evac, 1)
                    elif n == 5:
                        nc.scalar.copy(v[:, t, NB:AW], src[:, 0:AW - NB]).then_inc(proj_evac, 1)
                    else:
                        nc.scalar.activation(qg[:, t, NB * (n - 6):NB * (n - 5)], src, ACT.Sigmoid) \
                            .then_inc(proj_evac, 1)

                def qk_evac(i):
                    part, t = divmod(i, 2)
                    act.wait_ge(qkT_full, 4 * L + i + 1)
                    nc.scalar.copy(qkTc[:, 6 * part:6 * part + 6, P * t:P * t + P],
                                   psT[:, 0:AW].rearrange("p (c s) -> p c s", c=6)).then_inc(qkT_evac, 1)

                def softmax_exp(u):
                    act.wait_ge(nmx_ready, 8 * L + u + 1)
                    if 8 * L + u >= 2:
                        act.wait_ge(pT_full, 8 * L + u - 1)
                    nc.scalar.activation(p_sb[u % 2], s_sb[u % 2], ACT.Exp, bias=nmx[:, u % 2:u % 2 + 1], scale=QS,
                                         accum_out=den[:, 8 * L + u:8 * L + u + 1]).then_inc(p_ready, 1)

                if L == 0:
                    norm_std(0, lambda t: act.wait_ge(x_landed[t], 32))
                    rows_T_hi(0, (0, 1))
                    split(0)
                    rows_T_hi(0, (2, 3))
                    split(1)
                    for dst, src in late_consts:
                        act.dma_start(dst, src).then_inc(const_landed, 16)
                else:
                    norm_std(2, dense_complete)
                    rows_T_hi(3)
                for n in range(5):
                    split(2 * n + 2)
                    if n == 4:
                        qk_evac(0)
                    split(2 * n + 3)
                    if n == 4:
                        qk_evac(1)
                    evac(2 * n)
                    evac(2 * n + 1)
                    if n == 3:
                        for i in range(2):
                            act.wait_ge(fb_full, 2 * L + i + 1)
                            nc.scalar.copy(aT_hi[:, NB * i:NB * i + NB], ps[:, 6 + i, :]).then_inc(fb_hi, 1)
                qk_evac(2)
                evac(10)
                evac(11)
                qk_evac(3)
                for i in range(9):
                    split(12 + i)
                    if i >= 2 and i % 2 == 0:
                        evac(12 + i - 2)
                        evac(12 + i - 1)
                    if i < 8:
                        softmax_exp(i)
                split(21)
                act.wait_ge(oT_full, L + 1)
                nc.scalar.copy(os_hi[:, 0:NB], ps[:, 4, :]).then_inc(oT_hi, 1)
                split(22)
                split(23)
                K = 1 if L == 0 else 4
                rows_T_hi(K, (0, 1), by_half=True)
                split(24)
                rows_T_hi(K, (2, 3), by_half=True)
                split(25)
                split(26)
                split(27)

            def split_static(b):
                act.wait_ge(raw_landed[b % RAW], 16 * (b // RAW) + 16)
                if b >= SPL:
                    act.wait_ge(w_used, b - SPL + 1)
                nc.scalar.copy(whi[:, b % SPL, :], raw[:, b % RAW, :]).then_inc(hi_ready, 1)

            mixer(0)

            norm_std(1, lambda t: act.wait_ge(x_done, 2 * t + 2))
            rows_T_hi(2)
            split_static(DENSE0 + 2)
            split_static(DENSE0 + 3)

            def dense_silu(used):
                act.wait_ge(w_used, used)
                for t in range(NT):
                    nc.scalar.activation(ho[:, t, :], ps[:, t, :], ACT.Silu).then_inc(silu_done, 1)

            def dense_hiT(before_step):
                for t in range(NT):
                    act.wait_ge(aT_full, before_step + (t + 1))
                    nc.scalar.copy(aT_hi[:, NB * t:NB * t + NB], ps[:, 4 + t, :]).then_inc(aT_hi_done, 1)

            split_static(DENSE0 + 4)
            split_static(DENSE0 + 5)
            dense_silu(DENSE0 + 4)
            dense_hiT(0)
            with act.Fori(0, NSTEP - 1) as n:
                for i in range(2, 6):
                    split_loop(DENSE0 + 4 + i, 16 * n, 6 * n)
                dense_silu(n * 6 + (DENSE0 + 8))
                split_loop(DENSE0 + 4 + 6, 16 * n, 6 * n)
                dense_hiT(n * 2 + 2)
                split_loop(DENSE0 + 4 + 7, 16 * n, 6 * n)
            split_static(MIX1)
            split_static(MIX1 + 1)
            mixer(1)

            norm_std(3, lambda t: act.wait_ge(x_done, 4 + 2 * t + 2))
            for r in range(4):
                t, c = divmod(r, 2)
                act.wait_ge(rT_full, r + 1)
                nc.scalar.copy(routT[:, 4 * c:4 * c + 4, P * t:P * t + P],
                               ps[:, 4 + r % 2, :].rearrange("p (k s) -> p k s", k=4)).then_inc(rT_evac, 1)
            split_static(MOE0 + 2)
            nc.scalar.activation(warm[:, 5:6], eps[:], ACT.Exp).then_inc(warm_done, 1)
            act.wait_ge(exp_ready, 1)
            nc.scalar.activation(r1[:, :, 3:4], r1[:, :, 2:3], ACT.Exp).then_inc(exp_ready, 1)

            def gather_hi(k):
                act.wait_ge(g_full, k)
                nc.scalar.copy(hT_hi[:, 0:D], ps23).then_inc(g_hi, 1)

            gather_hi(1)
            act.wait_ge(njobs_ready, 1)
            n_jobs = act.value_load(njobs_i[0:1, 0:1], min_val=NE, max_val=2 * NE)
            with act.Fori(0, n_jobs) as j:
                l16, u42, u7 = act.snap(j * (16 * FF // RAW)), act.snap(j * FF), act.snap(j * NSTEP)

                def split(i):
                    split_loop(MOE0 + i, l16, u42)

                def silu(n):
                    act.wait_ge(w_used, u42 + (MOE0 + (4 if n == 0 else 6 * n + 2)))
                    nc.scalar.activation(ho[:, 0, :], ps[:, 0, :], ACT.Silu).then_inc(silu_done, 1)

                def hiT(n):
                    act.wait_ge(aT_full, u7 + (2 * NSTEP + n + 1))
                    nc.scalar.copy(aT_hi[:, 0:NB], ps[:, 4, :]).then_inc(aT_hi_done, 1)

                for i in range(3, 6):
                    split(i)
                silu(0)
                for n in range(1, NSTEP):
                    s = 6 * n - 2
                    split(s + 2)
                    hiT(n - 1)
                    if n == 2:
                        act.wait_ge(selT_full, j + 1)
                        nc.scalar.copy(selT[:], ps[:, 5, 0:SEQ]).then_inc(selT_ready, 1)
                    split(s + 3)
                    split(s + 4)
                    split(s + 5)
                    silu(n)
                    split(s + 6)
                    split(s + 7)
                hiT(NSTEP - 1)
                gather_hi(j + 2)
                with act.If(j + 1 < n_jobs):
                    split(FF)
                    split(FF + 1)
                for c in range(2):
                    act.wait_ge(w_used, u42 + (MOE0 + FF - 1 + c))
                    nc.scalar.copy(os_hi[:, NB * c:NB * c + NB], ps[:, 6 + c, :]).then_inc(yj_hi, 1)
                with act.If(j + 1 < n_jobs):
                    split(FF + 2)
            norm_std(4, lambda t: act.wait_ge(scat_added, n_jobs * 4 + (3 + t)))

        @block.gpsimd
        def _(pool):
            nc.gpsimd.memset(eps[:], EPS).then_inc(init_done, 1)
            nc.gpsimd.memset(selT[:].bitcast(F32), 0.0).then_inc(init_done, 1)
            pool.wait_ge(const_landed, 16 * 7)
            tmp_a = h[:, 0, 0:AW].rearrange("p (h d) -> p h d", d=HD)
            tmp_b = h[:, 1, 0:AW].rearrange("p (h d) -> p h d", d=HD)
            half = HD // 2
            step = 0
            for L in range(2):
                for i in range(4):
                    part, t = divmod(i, 2)
                    pool.wait_ge(proj_evac, NPROD * L + (6 if part == 0 else 8))
                    t_in = qg[:, t, AW * part:AW * part + AW].rearrange("p (h d) -> p h d", d=HD)
                    nh = AW // HD
                    cos = rope[:, t, 0:1, :].broadcast_to([P, nh, HD])
                    nsin = rope[:, t, 1:2, 0:half].broadcast_to([P, nh, half])
                    psin = rope[:, t, 1:2, half:HD].broadcast_to([P, nh, half])
                    if step:
                        pool.wait_ge(rope_done, 4 * L + i)
                    nc.gpsimd.tensor_tensor(tmp_a, t_in, cos, ALU.mult).then_inc(rope_step, 1)
                    nc.gpsimd.tensor_tensor(tmp_b[:, :, 0:half], t_in[:, :, half:HD], nsin, ALU.mult) \
                        .then_inc(rope_step, 1)
                    nc.gpsimd.tensor_tensor(tmp_b[:, :, half:HD], t_in[:, :, 0:half], psin, ALU.mult) \
                        .then_inc(rope_step, 1)
                    step += 3
                    pool.wait_ge(rope_step, step)
                    nc.gpsimd.tensor_tensor(t_in, tmp_a, tmp_b, ALU.add).then_inc(rope_done, 1)

        @block.vector
        def _(dve):
            def split_static(b):
                dve.wait_ge(hi_ready, b + 1)
                nc.vector.tensor_tensor(wlo[:, b % SPL, :], raw[:, b % RAW, :],
                                        whi[:, b % SPL, :].bitcast(F32), ALU.subtract).then_inc(lo_ready, 1)

            def split_loop(s, add):
                dve.wait_ge(hi_ready, add + (s + 1))
                nc.vector.tensor_tensor(wlo[:, s % SPL, :], raw[:, s % RAW, :],
                                        whi[:, s % SPL, :].bitcast(F32), ALU.subtract).then_inc(lo_ready, 1)

            def norm(N, K=None, after_tile=lambda t: None):
                dve.wait_ge(gain_landed, 16 * N + 16)
                for t in range(NT):
                    i = 2 * N + t
                    dve.wait_ge(std_ready, i + 1)
                    nc.vector.reciprocal(rstd[:, i:i + 1], std[:, i:i + 1]).then_inc(rstd_ready, 1)
                    dve.wait_ge(rstd_ready, i + 1)
                    for c in range(2):
                        cols = slice(NB * c, NB * c + NB)
                        nc.vector.scalar_tensor_tensor(h[:, t, cols], x[:, t, cols], rstd[:, i:i + 1], gain[:, cols],
                                                       ALU.mult, ALU.mult).then_inc(h_ready, 1)
                    if K is not None:
                        rows_T_lo(K, (2 * t, 2 * t + 1))
                    after_tile(t)

            def rows_T_lo(K, places, by_half=False):
                for r in places:
                    t, c = (r % 2, r // 2) if by_half else (r // 2, r % 2)
                    dve.wait_ge(hT_hi_done, 4 * K + r + 1)
                    view = lambda buf: buf.rearrange("p (k s) -> p k s", k=KD)[:, 4 * c:4 * c + 4, P * t:P * t + P]
                    nc.vector.tensor_tensor(view(hT_lo[:, :]), ps[:, 4 + r % 2, :].rearrange("p (k s) -> p k s", k=4),
                                            view(hT_hi[:, :].bitcast(F32)), ALU.subtract).then_inc(hT_lo_done, 1)

            def mixer(L):
                base = 0 if L == 0 else MIX1

                def split(m):
                    split_static(base + m)

                def row_max(u):
                    t = u // HG
                    dve.wait_ge(sc_full, 8 * L + u + 1)
                    if 8 * L + u >= 2:
                        dve.wait_ge(p_ready, 8 * L + u - 1)
                    nc.vector.tensor_tensor_reduce(s_sb[u % 2], ps[:, 6 + u % 2, :], mask[:, SEQ * t:SEQ * t + KEYS],
                                                   1.0, -3.0e38, ALU.add, ALU.max, mx[:, u % 2:u % 2 + 1]) \
                        .then_inc(sc_used, 1)
                    dve.wait_ge(sc_used, 8 * L + u + 1)
                    nc.vector.tensor_scalar(nmx[:, u % 2:u % 2 + 1], mx[:, u % 2:u % 2 + 1], -QS, None, ALU.mult) \
                        .then_inc(nmx_ready, 1)

                def copy_pT(u):
                    dve.wait_ge(pT_full, 8 * L + u + 1)
                    if 8 * L + u >= 2:
                        dve.wait_ge(pv_full, 8 * L + u - 1)
                    nc.vector.tensor_copy(pT[u % 2], ps[:, 4 + u % 2, :]).then_inc(pT_evac, 1)

                def normalise(u):
                    t, j = divmod(u, HG)
                    i = 8 * L + u
                    nc.vector.reciprocal(rden[:, i:i + 1], den[:, i:i + 1]).then_inc(rden_ready, 1)
                    dve.wait_ge(pv_full, i + 1)
                    dve.wait_ge(rden_ready, i + 1)
                    nc.vector.tensor_scalar(o[:, t, HD * j:HD * j + HD], pv_out(u),
                                            rden[:, i:i + 1], None, ALU.mult).then_inc(o_done, 1)

                norm(2 * L, 0 if L == 0 else 3, split if L == 0 else lambda t: None)
                for n in range(5):
                    split(2 * n + 2)
                    split(2 * n + 3)
                    if n == 2:
                        for g in range(FG):
                            dve.wait_ge(fa_full, FG * L + g + 1)
                            nc.vector.tensor_copy(fab[:, g, :], ps[:, 6 + g % 2, :]).then_inc(fa_evac, 1)
                    if n == 3:
                        for i in range(2):
                            dve.wait_ge(fb_hi, 2 * L + i + 1)
                            nc.vector.tensor_tensor(aT_lo[:, NB * i:NB * i + NB], ps[:, 6 + i, :],
                                                    aT_hi[:, NB * i:NB * i + NB].bitcast(F32), ALU.subtract) \
                                .then_inc(fb_lo, 1)
                dve.wait_ge(const_landed, 16 * 7)
                for i in range(9):
                    split(12 + i)
                    if i < 8:
                        row_max(i)
                    if i >= 1:
                        copy_pT(i - 1)
                    if i >= 2:
                        normalise(i - 2)
                normalise(7)
                split(21)
                dve.wait_ge(oT_hi, L + 1)
                nc.vector.tensor_tensor(os_lo[:, 0:NB], ps[:, 4, :], os_hi[:, 0:NB].bitcast(F32), ALU.subtract) \
                    .then_inc(oT_lo, 1)
                split(22)

                def zf_half(c):
                    for t in range(NT):
                        nc.vector.tensor_tensor(h[:, t, NB * c:NB * c + NB], ps[:, 2 * t + c, :],
                                                qg[:, t, NB * c:NB * c + NB], ALU.mult).then_inc(zf_done, 1)

                def z_half(c):
                    for t in range(NT):
                        i = 4 * L + 2 * c + t
                        if c == 1:
                            dve.wait_ge(z_ready, i - 1)
                        nc.vector.tensor_tensor(ho[:, t, :], ps[:, 4 + 2 * c + t, :],
                                                qg[:, t, D + NB * c:D + NB * c + NB], ALU.mult).then_inc(za_done, 1)
                        dve.wait_ge(za_done, i + 1)
                        dve.wait_ge(zf_done, i + 1)
                        nc.vector.tensor_tensor(h[:, t, NB * c:NB * c + NB], h[:, t, NB * c:NB * c + NB],
                                                ho[:, t, :], ALU.add).then_inc(z_ready, 1)

                K = 1 if L == 0 else 4
                dve.wait_ge(w_used, base + 21)
                zf_half(0)
                dve.wait_ge(ya_half, L + 1)
                z_half(0)
                zf_half(1)
                rows_T_lo(K, (0, 1), by_half=True)
                split(23)
                dve.wait_ge(w_used, base + 22)
                z_half(1)
                split(24)
                rows_T_lo(K, (2, 3), by_half=True)
                split(25)
                split(26)
                split(27)
                for t in range(NT):
                    if t == 0:
                        dve.wait_ge(xo_half, L + 1)
                    else:
                        dve.wait_ge(w_used, base + 26)
                    for c in range(2):
                        nc.vector.tensor_tensor(x[:, t, NB * c:NB * c + NB], x[:, t, NB * c:NB * c + NB],
                                                ps[:, 2 * t + c, :], ALU.add).then_inc(x_done, 1)
                dve.wait_ge(x_done, 4 * L + 4)

            for t in range(NT):
                dve.wait_ge(x_landed[t], 32)
            mixer(0)

            norm(1, 2)

            def dense_mul(k2, k):
                for t in range(NT):
                    dve.wait_ge(silu_done, k2 + (t + 1))
                    nc.vector.tensor_tensor(ho[:, t, :], ho[:, t, :], ps[:, 2 + t, :], ALU.mult) \
                        .then_inc(act_ready, 1)

            def dense_loT(before_step):
                for t in range(NT):
                    dve.wait_ge(aT_hi_done, before_step + (t + 1))
                    nc.vector.tensor_tensor(aT_lo[:, NB * t:NB * t + NB], ps[:, 4 + t, :],
                                            aT_hi[:, NB * t:NB * t + NB].bitcast(F32), ALU.subtract) \
                        .then_inc(aT_lo_done, 1)

            def dense_add(k2, used, c):
                for t in range(NT):
                    if t == 0:
                        dve.wait_ge(y_full, k2 + (c + 1))
                    else:
                        dve.wait_ge(w_used, used)
                    nc.vector.tensor_tensor(x[:, t, NB * c:NB * c + NB], x[:, t, NB * c:NB * c + NB],
                                            ps[:, 6 + t, :], ALU.add).then_inc(y_added, 1)

            for i in range(2, 6):
                split_static(DENSE0 + i)
            dense_mul(0, 0)
            dense_loT(0)
            with dve.Fori(0, NSTEP - 1) as n:
                for i in range(2, 6):
                    split_loop(DENSE0 + 4 + i, 6 * n)
                dense_mul(2 * n + 2, n)
                dense_add(n * 2, n * 6 + (DENSE0 + 9), 0)
                split_loop(DENSE0 + 4 + 6, 6 * n)
                dense_add(n * 2, n * 6 + (DENSE0 + 10), 1)
                dense_loT(n * 2 + 2)
                split_loop(DENSE0 + 4 + 7, 6 * n)
                dve.wait_ge(y_added, 4 * n + 4)
            split_static(MIX1)
            dense_add(2 * NSTEP - 2, DENSE0 + FF - 1, 0)
            split_static(MIX1 + 1)
            dense_add(2 * NSTEP - 2, DENSE0 + FF, 1)
            dve.wait_ge(y_added, 4 * NSTEP)
            mixer(1)

            norm(3)
            split_static(MOE0 + 2)
            nc.vector.memset(ones, 1.0).then_inc(init_done, 1)
            nc.vector.memset(comb[:, :, 0:1], 0.0).then_inc(init_done, 1)
            nc.vector.memset(os_hi[:].bitcast(F32), 0.0).then_inc(yj_lo, 1)
            nc.vector.memset(os_lo[:].bitcast(F32), 0.0).then_inc(yj_lo, 1)
            steps = [0]

            def chain(ins):
                steps[0] += 1
                ins.then_inc(route_step, 1)
                dve.wait_ge(route_step, steps[0])

            V = nc.vector
            lg, c1, one1, l2, c2, one2, msk, cmb = (rt[:, :, i, :] for i in range(8))
            m1, i1, dlt, e21, m2, i2, sm, wa = (r1[:, :, i:i + 1] for i in range(8))
            rev = iota[:, P:P + NE]
            rev2 = rev.rearrange("p (a e) -> p a e", a=1).broadcast_to([P, NT, NE])
            wide = lambda a: a.broadcast_to([P, NT, NE])

            dve.wait_ge(logit_full, 1)
            chain(V.tensor_tensor(lg, ps[:, 2:4, 0:NE],
                                  rb[:, :].rearrange("p (a e) -> p a e", a=1).broadcast_to([P, NT, NE]), ALU.add))

            def first_max(src, m, cand, idx, one):
                chain(V.tensor_reduce(m, src, AX_X, ALU.max))
                V.scalar_tensor_tensor(cand[:, 0, :], src[:, 0, :], m[:, 0, :], rev, ALU.is_ge, ALU.mult) \
                    .then_inc(route_step, 1)
                steps[0] += 1
                chain(V.scalar_tensor_tensor(cand[:, 1, :], src[:, 1, :], m[:, 1, :], rev, ALU.is_ge, ALU.mult))
                chain(V.tensor_reduce(idx, cand, AX_X, ALU.max))
                chain(V.tensor_tensor(one, rev2, wide(idx), ALU.is_equal))

            first_max(lg, m1, c1, i1, one1)
            chain(V.scalar_tensor_tensor(l2, one1, -3.0e38, lg, ALU.mult, ALU.add))
            first_max(l2, m2, c2, i2, one2)
            V.tensor_tensor(msk, one1, one2, ALU.add).then_inc(mask_ready, 1)
            V.tensor_tensor(dlt, m2, m1, ALU.subtract).then_inc(exp_ready, 1)
            dve.wait_ge(rank_full, 1)
            V.tensor_reduce(njobs_f[:, 0:1], ps[:, 2, 32:32 + NE], AX_X, ALU.max).then_inc(count_max, 1)
            dve.wait_ge(mask_ready, 1)
            chain(V.scalar_tensor_tensor(pos[:, :, 0:NE], ps[:, 2:4, 16:16 + NE], 1000.0, msk, ALU.add, ALU.mult))

            def build_sel(col):
                for t in range(NT):
                    V.tensor_scalar(sel[:, t, :], iota[:, 0:P], col(pos, t), None, ALU.is_equal).then_inc(sel_ready, 1)

            build_sel(lambda a, t: a[:, t, 0:1])
            chain(V.tensor_scalar(pos[:, :, NE:2 * NE], pos[:, :, 0:NE], -float(P), None, ALU.add))
            chain(V.memset(pos[:, :, 2 * NE:2 * NE + 1], -1.0))
            dve.wait_ge(count_max, 1)
            chain(V.tensor_scalar(njobs_f[:, 1:2], njobs_f[:, 0:1], P + 0.5, float(NE), ALU.is_gt, ALU.mult))
            chain(V.tensor_scalar(njobs_f[:, 2:3], njobs_f[:, 1:2], float(NE), None, ALU.add))
            V.tensor_copy(njobs_i[:], njobs_f[:, 2:3]).then_inc(njobs_ready, 1)
            dve.wait_ge(njobs_ready, 1)
            dve.wait_ge(exp_ready, 2)
            chain(V.tensor_scalar(sm, e21, 1.0, None, ALU.add))
            chain(V.reciprocal(wa, sm))
            chain(V.tensor_tensor(cmb, one2, wide(e21), ALU.mult))
            chain(V.tensor_tensor(cmb, cmb, one1, ALU.add))
            chain(V.tensor_tensor(cmb, cmb, wide(wa), ALU.mult))
            for r in range(2):
                chain(V.tensor_copy(comb[:, :, 1 + NE * r:1 + NE * r + NE], cmb))
            n_jobs = dve.value_load(njobs_i[0:1, 0:1], min_val=NE, max_val=2 * NE)

            def gather_lo(k):
                dve.wait_ge(g_hi, k)
                V.tensor_tensor(hT_lo[:, 0:D], ps23, hT_hi[:, 0:D].bitcast(F32), ALU.subtract).then_inc(g_lo, 1)

            def scatter_add(k4, col):
                for c in range(2):
                    for t in range(NT):
                        i = 2 * c + t
                        dve.wait_ge(scat_full, k4 + (i + 1))
                        V.scalar_tensor_tensor(x[:, t, NB * c:NB * c + NB], ps[:, 2 + t, :], col(comb, t),
                                               x[:, t, NB * c:NB * c + NB], ALU.mult, ALU.add) \
                            .then_inc(scat_added, 1)

            dve.wait_ge(init_done, 4)
            gather_lo(1)
            with dve.Fori(0, n_jobs) as j:
                u42, u7, u4 = dve.snap(j * FF), dve.snap(j * NSTEP), dve.snap(j * 4)

                def split(i):
                    split_loop(MOE0 + i, u42)

                def mul(n):
                    dve.wait_ge(silu_done, u7 + (2 * NSTEP + n + 1))
                    V.tensor_tensor(ho[:, 0, :], ho[:, 0, :], ps[:, 1, :], ALU.mult).then_inc(act_ready, 1)

                def loT(n):
                    dve.wait_ge(aT_hi_done, u7 + (2 * NSTEP + n + 1))
                    V.tensor_tensor(aT_lo[:, 0:NB], ps[:, 4, :], aT_hi[:, 0:NB].bitcast(F32), ALU.subtract) \
                        .then_inc(aT_lo_done, 1)

                for i in range(3, 6):
                    split(i)
                mul(0)
                scatter_add(u4, lambda a, t: a[:, t, bass.ds(j, 1)])
                for n in range(1, NSTEP):
                    s = 6 * n - 2
                    split(s + 2)
                    loT(n - 1)
                    split(s + 3)
                    split(s + 4)
                    split(s + 5)
                    mul(n)
                    if n == 3:
                        dve.wait_ge(selT_full, j + 1)
                        build_sel(lambda a, t: a[:, t, bass.ds(j + 1, 1)])
                    split(s + 6)
                    split(s + 7)
                loT(NSTEP - 1)
                gather_lo(j + 2)
                with dve.If(j + 1 < n_jobs):
                    split(FF)
                    split(FF + 1)
                for c in range(2):
                    dve.wait_ge(yj_hi, j * 2 + (c + 1))
                    V.tensor_tensor(os_lo[:, NB * c:NB * c + NB], ps[:, 6 + c, :],
                                    os_hi[:, NB * c:NB * c + NB].bitcast(F32), ALU.subtract).then_inc(yj_lo, 1)
                with dve.If(j + 1 < n_jobs):
                    split(FF + 2)
                dve.wait_ge(scat_added, u4 + 4)
            scatter_add(dve.snap(n_jobs * 4), lambda a, t: a[:, t, bass.ds(n_jobs, 1)])
            dve.wait_ge(scat_added, n_jobs * 4 + 4)
            norm(4)

        @block.tensor
        def _(pe):
            mm = nc.tensor.matmul

            def three(dst, a_hi, a_lo, b_hi, b_lo, start, stop):
                mm(dst, a_hi, b_hi, start=start, stop=False)
                mm(dst, a_lo, b_hi, start=False, stop=False)
                return mm(dst, a_hi, b_lo, start=False, stop=stop)

            def rows_T(K, r, t, c, src):
                if r >= 2:
                    pe.wait_ge(hT_lo_done, 4 * K + r - 1)
                for k in range(4):
                    last = nc.tensor.transpose(ps[:, 4 + r % 2, P * k:P * k + P],
                                               src[:, t, P * (4 * c + k):P * (4 * c + k) + P], ident[:])
                last.then_inc(hT_full, 1)

            def normed_T(K, N, t):
                for c in range(2):
                    pe.wait_ge(h_ready, 4 * N + 2 * t + c + 1)
                    rows_T(K, 2 * t + c, t, c, h)

            def mixer(L):
                base = 0 if L == 0 else MIX1

                K0 = 0 if L == 0 else 3

                def proj_block(m, n):
                    b = base + m
                    chunks = 8 if m == 10 else 4
                    cols = 256 if m == 10 else NB
                    first = m == 10 or (m % 2 == 0 if m < 10 else m % 2 == 1)
                    last_half = m == 10 or not first
                    k0 = 0 if first else 4
                    hi, lo = wblock(whi, b, SPL, chunks), wblock(wlo, b, SPL, chunks)
                    for t in range(NT):
                        if m == 0 and t == 0:
                            normed_T(K0, 2 * L, 0)
                        if t == 0:
                            pe.wait_ge(lo_ready, b + 1)
                        if m <= 1:
                            pe.wait_ge(hT_lo_done, 4 * K0 + 2 * t + m + 1)
                        q = 2 * n + t
                        if first and q >= 4:
                            pe.wait_ge(proj_evac, NPROD * L + (q - 3 if q < 12 else q - 1))
                        for k in range(chunks):
                            a = SEQ * (k0 + k) + P * t
                            ins = three(ps[:, proj_bank(q), 0:cols], hT_hi[:, a:a + P], hT_lo[:, a:a + P],
                                        hi[:, k, :], lo[:, k, :], first and k == 0, last_half and k == chunks - 1)
                            if m == 0 and t == 0 and k == 2:
                                normed_T(K0, 2 * L, 1)
                    ins.then_inc(w_used, 1)

                def fourier_a():
                    pe.wait_ge(proj_evac, NPROD * L + 2)
                    pe.wait_ge(dft_landed, 16 * L + 16)
                    pe.wait_ge(const_landed, 16 * 7)
                    for g in range(FG):
                        if g >= 2:
                            pe.wait_ge(fa_evac, FG * L + g - 1)
                        for t in range(NT):
                            ins = mm(ps[:, 6 + g % 2, :], ho[:, t, P * g:P * g + P], dftpos[:, t, :],
                                     start=t == 0, stop=t == NT - 1)
                        ins.then_inc(fa_full, 1)

                def fourier_b():
                    for i in range(2):
                        pe.wait_ge(fa_evac, FG * L + 4)
                        for g in (2 * i, 2 * i + 1):
                            dst = ps[:, 6 + i, SEQ * (g % 2):SEQ * (g % 2) + SEQ]
                            mm(dst, dftch[:, 0, :], fab[:, g, 0:SEQ], start=True, stop=False)
                            ins = mm(dst, dftch[:, 1, :], fab[:, g, SEQ:2 * SEQ], start=False, stop=True)
                        ins.then_inc(fb_full, 1)

                def qk_T(i):
                    part, t = divmod(i, 2)
                    pe.wait_ge(rope_done, 4 * L + i + 1)
                    if i:
                        pe.wait_ge(qkT_evac, 4 * L + i)
                    for c in range(6):
                        a = AW * part + P * c
                        ins = nc.tensor.transpose(psT[:, P * c:P * c + P], qg[:, t, a:a + P], ident[:])
                    ins.then_inc(qkT_full, 1)

                def key_blocks(t):
                    band, dil = [(0, 0), (0, 1)], [(1, t), (2, t)]
                    return band + dil if t == 0 else dil + band

                def scores(u):
                    t, j = divmod(u, HG)
                    if u == 0:
                        pe.wait_ge(qkT_evac, 4 * L + 4)
                        pe.wait_ge(fb_lo, 2 * L + 2)
                    elif u >= 2:
                        pe.wait_ge(sc_used, 8 * L + u - 1)
                    blocks = key_blocks(t)
                    for i, (g, kt) in enumerate(blocks):
                        if g == 0 and kt == 1:
                            continue
                        n = SEQ if g == 0 else P
                        head = HG * g + j
                        c, p0 = head // 2, HD * (head % 2)
                        ins = mm(ps[:, 6 + u % 2, P * i:P * i + n], qkTc[p0:p0 + HD, c, P * t:P * t + P],
                                 qkTc[p0:p0 + HD, 6 + c, P * kt:P * kt + n], start=True, stop=True)
                    ins.then_inc(sc_full, 1)

                def prob_T(u):
                    pe.wait_ge(p_ready, 8 * L + u + 1)
                    if u >= 2:
                        pe.wait_ge(pT_evac, 8 * L + u - 1)
                    for c in range(KEYS // P):
                        ins = nc.tensor.transpose(ps[:, 4 + u % 2, P * c:P * c + P], p_sb[u % 2][:, P * c:P * c + P],
                                                  ident[:])
                    ins.then_inc(pT_full, 1)

                def prob_v(u):
                    t, j = divmod(u, HG)
                    pe.wait_ge(pT_evac, 8 * L + u + 1)
                    if u < 2:
                        pe.wait_ge(proj_evac, NPROD * L + 11 + u)
                    elif u < 6:
                        pe.wait_ge(o_done, 8 * L + u - 1)
                    blocks = key_blocks(t)
                    for c, (g, kt) in enumerate(blocks):
                        head = HG * g + j
                        ins = mm(pv_out(u), pT[u % 2][:, P * c:P * c + P], v[:, kt, HD * head:HD * head + HD],
                                 start=c == 0, stop=c == len(blocks) - 1)
                    ins.then_inc(pv_full, 1)

                for m in range(11):
                    if m >= 8:
                        qk_T(m - 8)
                    proj_block(m, m // 2)
                    if m == 5:
                        fourier_a()
                    if m == 7:
                        fourier_b()
                def attention_T():
                    pe.wait_ge(o_done, 8 * L + 8)
                    for c in range(2):
                        for t in range(NT):
                            ins = nc.tensor.transpose(ps[:, 4, SEQ * c + P * t:SEQ * c + P * t + P],
                                                      o[:, t, P * c:P * c + P], ident[:])
                    ins.then_inc(oT_full, 1)

                qk_T(3)
                for i in range(10):
                    if i < 8:
                        scores(i)
                    if 1 <= i <= 8:
                        prob_T(i - 1)
                    if i >= 2:
                        prob_v(i - 2)
                    if i < 8:
                        proj_block(11 + i, 6 + i // 2)
                    else:
                        b = base + 11 + i
                        if i == 8:
                            pe.wait_ge(proj_evac, NPROD * L + 20)
                            pe.wait_ge(o_done, 8 * L + 6)
                        pe.wait_ge(lo_ready, b + 1)
                        hi, lo = wblock(whi, b, SPL, 2), wblock(wlo, b, SPL, 2)
                        for t in range(NT):
                            if i == 9 and t == 1:
                                attention_T()
                            for c in range(2):
                                for k in range(2):
                                    a = SEQ * (2 * (i - 8) + k) + P * t
                                    ins = three(ps[:, 2 * t + c, :], aT_hi[:, a:a + P], aT_lo[:, a:a + P],
                                                hi[:, k, NB * c:NB * c + NB], lo[:, k, NB * c:NB * c + NB],
                                                i == 8 and k == 0, i == 9 and k == 1)
                        ins.then_inc(w_used, 1)
                b = base + 21
                pe.wait_ge(oT_lo, L + 1)
                pe.wait_ge(lo_ready, b + 1)
                hi, lo = wblock(whi, b, SPL, 2), wblock(wlo, b, SPL, 2)
                for c in range(2):
                    for t in range(NT):
                        for k in range(2):
                            a = SEQ * k + P * t
                            ins = three(ps[:, 4 + 2 * c + t, :], os_hi[:, a:a + P], os_lo[:, a:a + P],
                                        hi[:, k, NB * c:NB * c + NB], lo[:, k, NB * c:NB * c + NB], k == 0, k == 1)
                    ins.then_inc(ya_half if c == 0 else w_used, 1)
                K = 1 if L == 0 else 4

                def z_T(c):
                    for t in range(NT):
                        pe.wait_ge(z_ready, 4 * L + 2 * c + t + 1)
                        rows_T(K, 2 * c + t, t, c, h)

                z_T(0)
                pe.wait_ge(zf_done, 4 * L + 4)
                for i in range(4):
                    b = base + 22 + i
                    pe.wait_ge(lo_ready, b + 1)
                    hi, lo = wblock(whi, b, SPL, 2), wblock(wlo, b, SPL, 2)
                    for t in range(NT):
                        if i % 2 == 0:
                            pe.wait_ge(hT_lo_done, 4 * K + i + t + 1)
                        for c in range(2):
                            for k in range(2):
                                a = SEQ * (2 * i + k) + P * t
                                ins = three(ps[:, 2 * t + c, :], hT_hi[:, a:a + P], hT_lo[:, a:a + P],
                                            hi[:, k, NB * c:NB * c + NB], lo[:, k, NB * c:NB * c + NB],
                                            i == 0 and k == 0, i == 3 and k == 1)
                        if i == 3 and t == 0:
                            ins.then_inc(xo_half, 1)
                    ins.then_inc(w_used, 1)
                    if i == 0:
                        z_T(1)

            pe.wait_ge(ident_landed, 16)
            mixer(0)

            def dense_up(s, add, first=False):
                for i in range(4):
                    pe.wait_ge(lo_ready, add + (s + i + 1))
                    hi, lo = wblock(whi, s + i, SPL, 4), wblock(wlo, s + i, SPL, 4)
                    for t in range(NT):
                        if first and i == 0 and t == 0:
                            normed_T(2, 1, 0)
                        if first and i <= 1:
                            pe.wait_ge(hT_lo_done, 8 + 2 * t + i + 1)
                        for k in range(4):
                            a = SEQ * (4 * (i % 2) + k) + P * t
                            ins = three(ps[:, 2 * (i // 2) + t, :], hT_hi[:, a:a + P], hT_lo[:, a:a + P],
                                        hi[:, k, :], lo[:, k, :], i % 2 == 0 and k == 0, i % 2 == 1 and k == 3)
                            if first and i == 0 and t == 0 and k == 2:
                                normed_T(2, 1, 1)
                    ins.then_inc(w_used, 1)

            def dense_down(s, add, steps2, added):
                for c in range(2):
                    pe.wait_ge(lo_ready, add + (s + c + 1))
                    hi, lo = wblock(whi, s + c, SPL, 4), wblock(wlo, s + c, SPL, 4)
                    for t in range(NT):
                        if c == 0:
                            pe.wait_ge(aT_lo_done, steps2 + (1 + t))
                        if c == 1:
                            pe.wait_ge(y_added, added + (t + 1))
                        for k in range(4):
                            a = NB * t + P * k
                            ins = three(ps[:, 6 + t, :], aT_hi[:, a:a + P], aT_lo[:, a:a + P],
                                        hi[:, k, :], lo[:, k, :], k == 0, k == 3)
                        ins.then_inc(y_full if t == 0 else w_used, 1)

            def dense_T(before_step):
                for t in range(NT):
                    pe.wait_ge(act_ready, before_step + (1 + t))
                    for k in range(4):
                        ins = nc.tensor.transpose(ps[:, 4 + t, P * k:P * k + P], ho[:, t, P * k:P * k + P], ident[:])
                    ins.then_inc(aT_full, 1)

            dense_up(DENSE0, 0, first=True)
            dense_T(0)
            with pe.Fori(0, NSTEP - 1) as n:
                n6, n4 = pe.snap(n * 6), pe.snap(n * 4)
                dense_up(DENSE0 + 4, n6)
                with pe.If(n > 0):
                    pe.wait_ge(y_added, n4)
                dense_down(DENSE0 + 8, n6, n * 2, n4)
                dense_T(n * 2 + 2)
            pe.wait_ge(y_added, 4 * NSTEP - 4)
            dense_down(DENSE0 + FF - 2, 0, 2 * NSTEP - 2, 4 * NSTEP - 4)
            mixer(1)

            for r in range(4):
                t, c = divmod(r, 2)
                pe.wait_ge(h_ready, 12 + r + 1)
                if r >= 2:
                    pe.wait_ge(rT_evac, r - 1)
                for k in range(4):
                    ins = nc.tensor.transpose(ps[:, 4 + r % 2, P * k:P * k + P],
                                              h[:, t, P * (4 * c + k):P * (4 * c + k) + P], ident[:])
                ins.then_inc(rT_full, 1)
            pe.wait_ge(rT_evac, 4)
            for t in range(NT):
                for k in range(KD):
                    ins = mm(ps[:, 2 + t, 0:NE], routT[:, k, P * t:P * t + P], rw[:, k, :],
                             start=k == 0, stop=k == KD - 1)
            ins.then_inc(logit_full, 1)
            pe.wait_ge(init_done, 4)
            pe.wait_ge(mask_ready, 1)
            msk = [rt[:, t, 6, :] for t in range(NT)]
            mm(ps[:, 2, 16:16 + NE], before[:], msk[0], start=True, stop=True)
            mm(ps[:, 3, 16:16 + NE], ones, msk[0], start=True, stop=False)
            mm(ps[:, 3, 16:16 + NE], before[:], msk[1], start=False, stop=True)
            mm(ps[:, 2, 32:32 + NE], ones, msk[0], start=True, stop=False)
            mm(ps[:, 2, 32:32 + NE], ones, msk[1], start=False, stop=True).then_inc(rank_full, 1)
            def gather(sel_count):
                pe.wait_ge(sel_ready, sel_count)
                for k in range(KD):
                    for t in range(NT):
                        ins = mm(ps23[:, P * k:P * k + P], h[:, t, P * k:P * k + P], sel[:, t, :],
                                 start=t == 0, stop=t == NT - 1)
                ins.then_inc(g_full, 1)

            def scatter(halves, added, last=False):
                for c in range(2):
                    pe.wait_ge(yj_lo, halves + (1 + c if last else 2))
                    for t in range(NT):
                        if c == 1:
                            pe.wait_ge(scat_added, added + (t + 1))
                        lhs = selT[:, P * t:P * t + P]
                        mm(ps[:, 2 + t, :], lhs, os_hi[:, NB * c:NB * c + NB], start=True, stop=False)
                        ins = mm(ps[:, 2 + t, :], lhs, os_lo[:, NB * c:NB * c + NB], start=False, stop=True)
                        ins.then_inc(scat_full, 1)

            gather(2)
            pe.wait_ge(njobs_ready, 1)
            n_jobs = pe.value_load(njobs_i[0:1, 0:1], min_val=NE, max_val=2 * NE)
            pe.wait_ge(init_done, 4)
            with pe.Fori(0, n_jobs) as j:
                u42, u7, u4 = pe.snap(j * FF), pe.snap(j * NSTEP), pe.snap(j * 4)

                def up(s):
                    for i in range(4):
                        b = MOE0 + s + i
                        pe.wait_ge(lo_ready, u42 + (b + 1))
                        hi, lo = wblock(whi, b, SPL, 4), wblock(wlo, b, SPL, 4)
                        for k in range(4):
                            a = P * (4 * (i % 2) + k)
                            ins = three(ps[:, i // 2, :], hT_hi[:, a:a + P], hT_lo[:, a:a + P],
                                        hi[:, k, :], lo[:, k, :], i % 2 == 0 and k == 0, i % 2 == 1 and k == 3)
                        ins.then_inc(w_used, 1)

                def hidden_T(n):
                    pe.wait_ge(act_ready, u7 + (2 * NSTEP + n + 1))
                    for k in range(4):
                        ins = nc.tensor.transpose(ps[:, 4, P * k:P * k + P], ho[:, 0, P * k:P * k + P], ident[:])
                    ins.then_inc(aT_full, 1)

                def down(n, s):
                    pe.wait_ge(aT_lo_done, u7 + (2 * NSTEP + n + 1))
                    for c in range(2):
                        b = MOE0 + s + c
                        pe.wait_ge(lo_ready, u42 + (b + 1))
                        hi, lo = wblock(whi, b, SPL, 4), wblock(wlo, b, SPL, 4)
                        for k in range(4):
                            ins = three(ps[:, 6 + c, :], aT_hi[:, P * k:P * k + P], aT_lo[:, P * k:P * k + P],
                                        hi[:, k, :], lo[:, k, :], n == 0 and k == 0, n == NSTEP - 1 and k == 3)
                        ins.then_inc(w_used, 1)

                pe.wait_ge(g_lo, j + 1)
                up(0)
                scatter(j * 2, u4)
                hidden_T(0)
                for n in range(1, NSTEP):
                    s = 6 * n - 2
                    up(s)
                    if n == 1:
                        for t in range(NT):
                            ins = nc.tensor.transpose(ps[:, 5, P * t:P * t + P], sel[:, t, :], ident[:])
                        ins.then_inc(selT_full, 1)
                    down(n - 1, s + 4)
                    hidden_T(n)
                pe.wait_ge(scat_added, u4 + 4)
                gather(2 * j + 4)
                down(NSTEP - 1, FF - 2)
            scatter(n_jobs * 2, pe.snap(n_jobs * 4), last=True)


def _constants():
    import numpy as np
    f = np.float32
    tok = (RES * np.arange(HALF)[None, :] + np.arange(RES)[:, None]).reshape(SEQ)
    s = tok.astype(np.float64)
    ang = 2 * np.pi * np.outer(s, s) / SEQ
    pos = np.concatenate([np.cos(ang), np.sin(ang)], 1) / np.sqrt(SEQ)
    c = np.arange(P, dtype=np.float64)
    angc = 2 * np.pi * np.outer(c, c) / P
    ch = np.stack([np.cos(angc), -np.sin(angc)], 1) / np.sqrt(P)
    no = f(-1e30)
    apart = tok[:, None] - tok[None, :]
    band = np.where(np.abs(apart) <= HD, f(0), no).reshape(NT, P, SEQ)
    dil = [np.where(apart[:P, :P] % d == 0, f(0), no) for d in (4, 16)]
    mask = np.concatenate([band[0], dil[0], dil[1], band[1]], 1).astype(f)
    half = HD // 2
    inv = f(10000.0) ** (-np.arange(half, dtype=f) * f(2.0) / f(HD))
    a = (tok.astype(f)[:, None] * inv[None, :].astype(f)).astype(f)
    co, si = np.cos(a), np.sin(a)
    rope = np.stack([np.concatenate([co, co], 1), np.concatenate([-si, si], 1)], 1)
    rope = rope.reshape(NT, P, 2, HD).transpose(1, 0, 2, 3)
    return {
        "c_ident": np.eye(P, dtype=f),
        "c_dftpos": pos.reshape(NT, P, NB).transpose(1, 0, 2).astype(f),
        "c_dftch": ch.astype(f),
        "c_mask": mask,
        "c_rope": rope.astype(f),
        "c_iota": np.tile(np.concatenate([1000 + np.arange(P), NE - np.arange(NE)]).astype(f), (P, 1)),
        "c_before": np.triu(np.ones((P, P), f), 1),
    }


_INS = ["x", "ln_mix", "w_in", "w_fourier", "w_attn", "w_out", "ln_ffn", "dense_w1", "dense_w3", "dense_w2",
        "router_w", "router_b", "moe_w1", "moe_w3", "moe_w2", "ln_final"]


def kernel(**inputs):
    import numpy as np
    import concourse.bacc as bacc
    from concourse.bass_utils import run_bass_kernel_spmd

    nc = bacc.Bacc("TRN2", target_bir_lowering=False, num_devices=1)
    arrays, args = {}, []
    feeds = {name: np.asarray(inputs[name]) for name in _INS}
    feeds.update(_constants())
    for name, a in feeds.items():
        a = np.ascontiguousarray(a)
        arrays[f"in_{name}"] = a
        args.append(nc.dram_tensor(f"in_{name}", a.shape, mybir.dt.from_np(a.dtype), kind="ExternalInput").ap())
    args.append(nc.dram_tensor("out_0", (1, SEQ, D), F32, kind="ExternalOutput").ap())
    build(nc, *args)
    r = run_bass_kernel_spmd(nc, [arrays], core_ids=[0])
    return r.results[0]["out_0"]
```

```python
from contextlib import ExitStack, nullcontext

import concourse.bass as bass
from concourse import mybir

F32 = mybir.dt.float32
F32R = mybir.dt.float32r
I32 = mybir.dt.int32
ALU = mybir.AluOpType
ACT = mybir.ActivationFunctionType
AX_X = mybir.AxisListType.X

P = 128
D = 1024
SEQ = 256
NT = SEQ // P
KD = D // P
NB = 512
FG = 4
HG = 4
HD = 64
NG = 3
AW = NG * HG * HD
FFN = 3584
NSTEP = FFN // NB
NE = 8
RAW = 6
AHEAD = 3
BESIDE = (3, 10, 17, 24, 31, 32)
SPL = 3
BLK = 2048
MIX = 26
FF = 6 * NSTEP
DENSE0 = MIX
MIX1 = MIX + FF
MOE0 = 2 * MIX + FF
EPS = 1e-6
QS = HD ** -0.5
NPROD = 20
RES = 4
HALF = SEQ // RES
KEYS = SEQ + 2 * P


def build(nc, x_in, ln_mix, w_in, w_fourier, w_attn, w_out, ln_ffn, dense_w1, dense_w3, dense_w2,
          router_w, router_b, moe_w1, moe_w3, moe_w2, ln_final,
          c_ident, c_dftpos, c_dftch, c_mask, c_rope, c_iota, c_before, out):
    with ExitStack() as ctx:
        def sb(name, shape, dt=F32):
            return ctx.enter_context(nc.sbuf_tensor(name, shape, dt))

        def sem(name):
            return ctx.enter_context(nc.semaphore(name))

        raw = sb("raw", [P, RAW, BLK])
        whi = sb("whi", [P, SPL, BLK], F32R)
        wlo = sb("wlo", [P, SPL, BLK], F32R)
        x = sb("x", [P, NT, D])
        h = sb("h", [P, NT, D])
        hT_hi = sb("hT_hi", [P, KD * SEQ], F32R)
        hT_lo = sb("hT_lo", [P, KD * SEQ], F32R)
        aT_hi = sb("aT_hi", [P, NT * NB], F32R)
        aT_lo = sb("aT_lo", [P, NT * NB], F32R)
        ho = sb("ho", [P, NT, NB])
        qg = sb("qg", [P, NT, 2 * D])
        v = sb("v", [P, NT, AW])
        qkT = sb("qkT", [P, 3072])
        att = sb("att", [P, 6 * KEYS])
        os_hi = sb("os_hi", [P, D], F32R)
        os_lo = sb("os_lo", [P, D], F32R)
        ident = sb("ident", [P, P])
        dftch = sb("dftch", [P, 2, P])
        mask = sb("mask", [P, 2 * SEQ + 2 * P])
        rope = sb("rope", [P, NT, 2, HD])
        iota = sb("iota", [P, P + NE])
        before = sb("before", [P, P])
        rw = sb("rw", [P, KD, NE])
        rb = sb("rb", [P, NE])
        sel = sb("sel", [P, NT, P])
        selT = sb("selT", [P, SEQ], F32R)
        ssq = sb("ssq", [P, 5 * NT])
        std = sb("std", [P, 5 * NT])
        rstd = sb("rstd", [P, 5 * NT])
        eps = sb("eps", [P, 1])
        warm = sb("warm", [P, 8])
        mx = sb("mx", [P, 2])
        nmx = sb("nmx", [P, 2])
        den = sb("den", [P, 16])
        rden = sb("rden", [P, 16])
        njobs_f = sb("njobs_f", [P, 4])
        njobs_i = sb("njobs_i", [P, 1], I32)

        ps = ctx.enter_context(nc.psum_tensor("ps", [P, 8, NB], F32))

        gain = att[:, 0:D]
        fab = att[:, 0:FG * NB].rearrange("p (g c) -> p g c", g=FG)
        s_sb, p_sb, pT = ([att[:, KEYS * (2 * i + b):KEYS * (2 * i + b) + KEYS] for b in range(2)] for i in range(3))
        o = h[:, 0, 0:NT * HG * HD].rearrange("p (t c) -> p t c", t=NT)
        dftpos = qkT[:, 0:NT * NB].rearrange("p (t c) -> p t c", t=NT)
        qkTc = qkT[:, :].rearrange("p (c s) -> p c s", c=12)
        routT = qg[:, :, :].rearrange("p a b -> p (a b)")[:, 0:KD * SEQ].rearrange("p (k s) -> p k s", k=KD)
        psT = ps[:, 4:6, :].rearrange("p b c -> p (b c)")
        ps23 = ps[:, 2:4, :].rearrange("p b c -> p (b c)")

        v_end = v[:, :, :].rearrange("p t c -> p (t c)")
        rt = v_end[:, 0:8 * NT * NE].rearrange("p (t i e) -> p t i e", t=NT, i=8)
        r1 = v_end[:, 128:128 + 8 * NT].rearrange("p (t i) -> p t i", t=NT)
        JC = 2 * NE + 1
        comb = v_end[:, 144:144 + NT * JC].rearrange("p (t j) -> p t j", t=NT)
        pos = v_end[:, 192:192 + NT * JC].rearrange("p (t j) -> p t j", t=NT)
        ones = v_end[:, 256:256 + P]

        as_chunks = lambda buf: buf.rearrange("p (k c) -> p k c", c=NB)
        qg_flat = qg[:, :, :].rearrange("p a b -> p (a b)")
        spare = [
            [as_chunks(qkT[:, 0:BLK])],
            [as_chunks(att[:, D:D + BLK])],
            [as_chunks(qg_flat[:, BLK:2 * BLK])],
            [as_chunks(v_end[:, 384:384 + 2 * NB]), as_chunks(ho[:, 1, :]), as_chunks(mask[:, 0:NB])],
            [as_chunks(att[:, 0:D]), as_chunks(qkT[:, BLK:BLK + D])],
            [as_chunks(qg_flat[:, 0:BLK])],
        ]

        x_landed = [sem(f"x_landed{t}") for t in range(NT)]
        ident_landed = sem("ident_landed")
        const_landed = sem("const_landed")
        gain_landed = sem("gain_landed")
        dft_landed = sem("dft_landed")
        raw_landed = [sem(f"raw_landed{i}") for i in range(RAW)]
        spare_landed = [sem(f"spare_landed{i}") for i in range(RAW)]
        hi_ready = sem("hi_ready")
        lo_ready = sem("lo_ready")
        half0_hi = sem("half0_hi")
        half0_lo = sem("half0_lo")
        w_used = sem("w_used")
        init_done = sem("init_done")
        ssq_ready = sem("ssq_ready")
        std_ready = sem("std_ready")
        rstd_ready = sem("rstd_ready")
        warm_done = sem("warm_done")
        h_ready = sem("h_ready")
        hT_full = sem("hT_full")
        hT_hi_done = sem("hT_hi_done")
        hT_lo_done = sem("hT_lo_done")
        proj_evac = sem("proj_evac")
        rope_step = sem("rope_step")
        rope_done = sem("rope_done")
        qkT_full = sem("qkT_full")
        qkT_evac = sem("qkT_evac")
        fa_full = sem("fa_full")
        fa_evac = sem("fa_evac")
        fb_full = sem("fb_full")
        fb_hi = sem("fb_hi")
        fb_lo = sem("fb_lo")
        sc_full = sem("sc_full")
        sc_used = sem("sc_used")
        nmx_ready = sem("nmx_ready")
        p_ready = sem("p_ready")
        pT_full = sem("pT_full")
        pT_evac = sem("pT_evac")
        pv_full = sem("pv_full")
        rden_ready = sem("rden_ready")
        o_done = sem("o_done")
        oT_full = sem("oT_full")
        oT_hi = sem("oT_hi")
        oT_lo = sem("oT_lo")
        ya_half = sem("ya_half")
        xo_half = sem("xo_half")
        zf_done = sem("zf_done")
        za_done = sem("za_done")
        z_ready = sem("z_ready")
        x_done = sem("x_done")
        silu_done = sem("silu_done")
        act_ready = sem("act_ready")
        aT_full = sem("aT_full")
        aT_hi_done = sem("aT_hi_done")
        aT_lo_done = sem("aT_lo_done")
        y_full = sem("y_full")
        y_added = sem("y_added")
        rT_full = sem("rT_full")
        rT_evac = sem("rT_evac")
        logit_full = sem("logit_full")
        exp_ready = sem("exp_ready")
        route_step = sem("route_step")
        mask_ready = sem("mask_ready")
        rank_full = sem("rank_full")
        count_max = sem("count_max")
        njobs_ready = sem("njobs_ready")
        sel_ready = sem("sel_ready")
        g_full = sem("g_full")
        g_hi = sem("g_hi")
        g_lo = sem("g_lo")
        yj_hi = sem("yj_hi")
        yj_lo = sem("yj_lo")
        selT_full = sem("selT_full")
        selT_ready = sem("selT_ready")
        scat_full = sem("scat_full")
        scat_added = sem("scat_added")
        out_done = sem("out_done")

        def proj_bank(q):
            return q % 4 if q < 12 else q % 2

        def pv_out(u):
            return ps[:, 2 + u % 2 if u < 6 else u, 0:HD]

        def by_residue(rows):
            return rows[0].rearrange("(i r) d -> r i d", r=RES)

        def k_rows(w):
            return w.rearrange("(k p) n -> p k n", p=P)

        def mix_src(L, m):
            wi = k_rows(w_in[L])
            if m < 10:
                return wi[:, 4 * (m % 2):4 * (m % 2) + 4, NB * (m // 2):NB * (m // 2) + NB], 4
            if m == 10:
                return wi[:, :, 2560:2816], 8
            if m < 19:
                a = 2816 + NB * ((m - 11) // 2)
                half = (m - 11) % 2
                return wi[:, 4 * half:4 * half + 4, a:a + NB], 4
            if m < 21:
                return k_rows(w_fourier[L])[:, 2 * (m - 19):2 * (m - 19) + 2, :], 2
            if m == 21:
                return k_rows(w_attn[L]), 2
            return k_rows(w_out[L])[:, 2 * (m - 22):2 * (m - 22) + 2, :], 2

        def wblock(buf, b_static, n, chunks):
            return buf[:, b_static % n, :].rearrange("p (k c) -> p k c", k=chunks)

        always = nullcontext

        block = ctx.enter_context(nc.Block())

        @block.sync
        def _(sp):
            def load(b, b_static, src, chunks, first=False):
                if not first:
                    sp.wait_ge(lo_ready, b - RAW + 1)
                sp.dma_start(wblock(raw, b_static, RAW, chunks), src).then_inc(raw_landed[b_static % RAW], 16)

            def load_gain(src):
                sp.dma_start(gain, src.partition_broadcast(P)).then_inc(gain_landed, 16)

            def load_x(t):
                for r in range(2):
                    sp.dma_start(x[HALF * r:HALF * r + HALF, t, :], by_residue(x_in)[2 * t + r]) \
                        .then_inc(x_landed[t], 16)

            load_x(0)
            load_gain(ln_mix[0])
            for L in range(2):
                base = 0 if L == 0 else MIX1
                if L == 1:
                    sp.wait_ge(h_ready, 8)
                    load_gain(ln_mix[1])
                for m in range(MIX):
                    if m == 4:
                        if L == 1:
                            sp.wait_ge(pv_full, 8)
                        sp.dma_start(dftpos, c_dftpos).then_inc(dft_landed, 16)
                    src, chunks = mix_src(L, m)
                    load(base + m, base + m, src, chunks, first=base + m < RAW)
                    if L == 0 and m == 0:
                        load_x(1)
                    if L == 0 and m == 5:
                        for dst, table in ((dftch[:], c_dftch), (mask[:], c_mask), (rope[:], c_rope),
                                           (iota[:], c_iota), (before[:], c_before), (rw[:], k_rows(router_w[0])),
                                           (rb[:], router_b[0].partition_broadcast(P))):
                            sp.dma_start(dst, table).then_inc(const_landed, 16)
                sp.wait_ge(pv_full, 8 * L + 8)
                load_gain(ln_ffn[L])
                if L == 0:
                    w1, w3, w2 = k_rows(dense_w1[0]), k_rows(dense_w3[0]), k_rows(dense_w2[0])
                    for i in range(4):
                        w = w1 if i < 2 else w3
                        load(DENSE0 + i, DENSE0 + i, w[:, 4 * (i % 2):4 * (i % 2) + 4, 0:NB], 4)
                    with sp.Fori(1, NSTEP) as n:
                        for i in range(6):
                            s = DENSE0 + 4 + i
                            if i < 4:
                                w = w1 if i < 2 else w3
                                src = w[:, 4 * (i % 2):4 * (i % 2) + 4, bass.ds(n * NB, NB)]
                            else:
                                src = w2[:, bass.ds(4 * n - 4, 4), NB * (i - 4):NB * (i - 4) + NB]
                            load(DENSE0 - 2 + 6 * n + i, s, src, 4)
                    for i in range(2):
                        b = DENSE0 + 6 * NSTEP - 2 + i
                        load(b, b, w2[:, 4 * NSTEP - 4:4 * NSTEP, NB * i:NB * i + NB], 4)

            def expert_src(e, i):
                rows = lambda w: w[0][bass.ds(e, 1)].rearrange("e (k p) n -> p (e k) n", p=P)
                n, q = divmod(i + 2, 6)
                if i < 4:
                    n, q = 0, i
                if i >= FF - 2:
                    n, q = NSTEP, 4 + i - (FF - 2)
                if q < 4:
                    return rows(moe_w1 if q < 2 else moe_w3)[:, 4 * (q % 2):4 * (q % 2) + 4, NB * n:NB * n + NB]
                return rows(moe_w2)[:, 4 * n - 4:4 * n, NB * (q - 4):NB * (q - 4) + NB]

            def load_expert(job, e):
                for i in range(FF):
                    load(FF * job + (MOE0 + i), MOE0 + i, expert_src(e, i), 4)

            def load_spare(r):
                src, k = expert_src(AHEAD, BESIDE[r]), 0
                for view in spare[r]:
                    n = view.shape[1]
                    sp.dma_start(view, src[:, k:k + n, :]).then_inc(spare_landed[r], 16)
                    k += n

            for i in range(6):
                load(MOE0 + i, MOE0 + i, expert_src(0, i), 4)
            load_spare(0)
            load_spare(1)
            sp.wait_ge(z_ready, 8)
            load_spare(2)
            load_spare(3)
            sp.wait_ge(h_ready, 16)
            load_spare(4)
            load(MOE0 + 6, MOE0 + 6, expert_src(0, 6), 4)
            sp.wait_ge(logit_full, 1)
            load_spare(5)
            for i in range(7, FF):
                load(MOE0 + i, MOE0 + i, expert_src(0, i), 4)
            with sp.Fori(1, AHEAD) as e:
                load_expert(e, e)
            for i in range(FF):
                if i in BESIDE:
                    continue
                b = MOE0 + FF * AHEAD + i
                back = 2 * RAW if i - RAW in BESIDE else RAW
                sp.wait_ge(lo_ready, b - back + 1)
                sp.dma_start(wblock(raw, b, RAW, 4), expert_src(AHEAD, i)).then_inc(raw_landed[b % RAW], 16)
            with sp.Fori(AHEAD + 1, NE) as e:
                load_expert(e, e)
            sp.wait_ge(njobs_ready, 1)
            n_jobs = sp.value_load(njobs_i[0:1, 0:1], min_val=NE, max_val=2 * NE)
            with sp.If(n_jobs > NE):
                with sp.Fori(0, NE) as e2:
                    load_expert(e2 + NE, e2)
            load_gain(ln_final)
            for t in range(NT):
                sp.wait_ge(h_ready, 18 + 2 * t)
                for r in range(2):
                    sp.dma_start(by_residue(out)[2 * t + r], h[HALF * r:HALF * r + HALF, t, :]).then_inc(out_done, 16)
            sp.wait_ge(out_done, 64)

        @block.scalar
        def _(act):
            def split_loop(s, landed_add, used_add):
                act.wait_ge(raw_landed[s % RAW], landed_add + (16 * (s // RAW) + 16))
                act.wait_ge(w_used, used_add + (s - SPL + 1))
                nc.scalar.copy(whi[:, s % SPL, :], raw[:, s % RAW, :]).then_inc(hi_ready, 1)

            def norm_std(N, x_complete, tiles=range(NT)):
                if 0 in tiles:
                    act.wait_ge(init_done, 1)
                    nc.scalar.activation(warm[:, N:N + 1], eps[:], ACT.Sqrt).then_inc(warm_done, 1)
                for t in tiles:
                    x_complete(t)
                    i = 2 * N + t
                    nc.scalar.activation(h[:, t, :], x[:, t, :], ACT.Square, accum_out=ssq[:, i:i + 1]) \
                        .then_inc(ssq_ready, 1)
                    act.wait_ge(ssq_ready, i + 1)
                    nc.scalar.activation(std[:, i:i + 1], ssq[:, i:i + 1], ACT.Sqrt, bias=eps[:], scale=1.0 / D) \
                        .then_inc(std_ready, 1)

            def rows_T_hi(K, places=range(4), by_half=False):
                for r in places:
                    t, c = (r % 2, r // 2) if by_half else (r // 2, r % 2)
                    act.wait_ge(hT_full, 4 * K + r + 1)
                    dst = hT_hi[:, :].rearrange("p (k s) -> p k s", k=KD)[:, 4 * c:4 * c + 4, P * t:P * t + P]
                    nc.scalar.copy(dst, ps[:, 4 + r % 2, :].rearrange("p (k s) -> p k s", k=4)) \
                        .then_inc(hT_hi_done, 1)

            act.dma_start(ident[:], c_ident).then_inc(ident_landed, 16)

            def dense_complete(t):
                act.wait_ge(y_added, 4 * NSTEP - 4 + 2 * t + 2)

            def mixer(L):
                base = 0 if L == 0 else MIX1

                def split(m):
                    split_static(base + m)

                def evac(q):
                    n, t = divmod(q, 2)
                    last = 2 * n + 1 if n < 5 else 2 * n
                    act.wait_ge(w_used, base + last + 1)
                    src = ps[:, proj_bank(q), :]
                    if n == 0:
                        nc.scalar.copy(ho[:, t, :], src).then_inc(proj_evac, 1)
                    elif n < 4:
                        nc.scalar.copy(qg[:, t, NB * (n - 1):NB * n], src).then_inc(proj_evac, 1)
                    elif n == 4:
                        nc.scalar.copy(v[:, t, 0:NB], src).then_inc(proj_evac, 1)
                    elif n == 5:
                        nc.scalar.copy(v[:, t, NB:AW], src[:, 0:AW - NB]).then_inc(proj_evac, 1)
                    else:
                        nc.scalar.activation(qg[:, t, NB * (n - 6):NB * (n - 5)], src, ACT.Sigmoid) \
                            .then_inc(proj_evac, 1)

                def qk_evac(i):
                    part, t = divmod(i, 2)
                    act.wait_ge(qkT_full, 4 * L + i + 1)
                    nc.scalar.copy(qkTc[:, 6 * part:6 * part + 6, P * t:P * t + P],
                                   psT[:, 0:AW].rearrange("p (c s) -> p c s", c=6)).then_inc(qkT_evac, 1)

                def softmax_exp(u):
                    act.wait_ge(nmx_ready, 8 * L + u + 1)
                    if 8 * L + u >= 2:
                        act.wait_ge(pT_full, 8 * L + u - 1)
                    nc.scalar.activation(p_sb[u % 2], s_sb[u % 2], ACT.Exp, bias=nmx[:, u % 2:u % 2 + 1], scale=QS,
                                         accum_out=den[:, 8 * L + u:8 * L + u + 1]).then_inc(p_ready, 1)

                if L == 0:
                    x_there = lambda t: act.wait_ge(x_landed[t], 32)
                    norm_std(0, x_there, (0,))
                    rows_T_hi(0, (0, 1))
                    act.wait_ge(raw_landed[0], 16)
                    nc.scalar.copy(whi[:, 0, 0:BLK // 2], raw[:, 0, 0:BLK // 2]).then_inc(half0_hi, 1)
                    nc.scalar.copy(whi[:, 0, BLK // 2:BLK], raw[:, 0, BLK // 2:BLK]).then_inc(hi_ready, 1)
                    norm_std(0, x_there, (1,))
                    split(1)
                    rows_T_hi(0, (2, 3))
                else:
                    norm_std(2, dense_complete, (0,))
                    split(1)
                    rows_T_hi(3, (0, 1))
                    norm_std(2, dense_complete, (1,))
                    rows_T_hi(3, (2, 3))
                for n in range(5):
                    split(2 * n + 2)
                    if n == 4:
                        qk_evac(0)
                    split(2 * n + 3)
                    if n == 4:
                        qk_evac(1)
                    evac(2 * n)
                    evac(2 * n + 1)
                    if n == 3:
                        for i in range(2):
                            act.wait_ge(fb_full, 2 * L + i + 1)
                            nc.scalar.copy(aT_hi[:, NB * i:NB * i + NB], ps[:, 6 + i, :]).then_inc(fb_hi, 1)
                qk_evac(2)
                evac(10)
                evac(11)
                qk_evac(3)
                for i in range(9):
                    if i >= 2 and i % 2 == 0:
                        evac(12 + i - 2)
                        evac(12 + i - 1)
                    split(12 + i)
                    if i < 8:
                        softmax_exp(i)
                split(21)
                act.wait_ge(oT_full, L + 1)
                nc.scalar.copy(os_hi[:, 0:NB], ps[:, 4, :]).then_inc(oT_hi, 1)
                split(22)
                split(23)
                K = 1 if L == 0 else 4
                rows_T_hi(K, (0, 1), by_half=True)
                split(24)
                rows_T_hi(K, (2, 3), by_half=True)
                split(25)
                split(26)

            def split_static(b):
                act.wait_ge(raw_landed[b % RAW], 16 * (b // RAW) + 16)
                if b >= SPL:
                    act.wait_ge(w_used, b - SPL + 1)
                nc.scalar.copy(whi[:, b % SPL, :], raw[:, b % RAW, :]).then_inc(hi_ready, 1)

            mixer(0)

            norm_std(1, lambda t: act.wait_ge(x_done, 2), (0,))
            split_static(DENSE0 + 1)
            rows_T_hi(2, (0, 1))
            norm_std(1, lambda t: act.wait_ge(x_done, 4), (1,))
            rows_T_hi(2, (2, 3))
            split_static(DENSE0 + 2)
            split_static(DENSE0 + 3)

            def dense_silu(used):
                act.wait_ge(w_used, used)
                for t in range(NT):
                    nc.scalar.activation(ho[:, t, :], ps[:, t, :], ACT.Silu).then_inc(silu_done, 1)

            def dense_hiT(before_step):
                for t in range(NT):
                    act.wait_ge(aT_full, before_step + (t + 1))
                    nc.scalar.copy(aT_hi[:, NB * t:NB * t + NB], ps[:, 4 + t, :]).then_inc(aT_hi_done, 1)

            split_static(DENSE0 + 4)
            split_static(DENSE0 + 5)
            dense_silu(DENSE0 + 4)
            dense_hiT(0)
            with act.Fori(0, NSTEP - 1) as n:
                for i in range(2, 6):
                    split_loop(DENSE0 + 4 + i, 16 * n, 6 * n)
                dense_silu(n * 6 + (DENSE0 + 8))
                split_loop(DENSE0 + 4 + 6, 16 * n, 6 * n)
                split_loop(DENSE0 + 4 + 7, 16 * n, 6 * n)
                dense_hiT(n * 2 + 2)
            split_static(MIX1)
            mixer(1)

            for t in range(NT):
                norm_std(3, lambda t: act.wait_ge(x_done, 4 + 2 * t + 2), (t,))
                for c in range(2):
                    r = 2 * t + c
                    act.wait_ge(rT_full, r + 1)
                    nc.scalar.copy(routT[:, 4 * c:4 * c + 4, P * t:P * t + P],
                                   ps[:, 4 + r % 2, :].rearrange("p (k s) -> p k s", k=4)).then_inc(rT_evac, 1)
            nc.scalar.activation(warm[:, 5:6], eps[:], ACT.Exp).then_inc(warm_done, 1)
            split_static(MOE0 + 1)
            split_static(MOE0 + 2)
            act.wait_ge(exp_ready, 1)
            nc.scalar.activation(r1[:, :, 3:4], r1[:, :, 2:3], ACT.Exp).then_inc(exp_ready, 1)

            def gather_hi(k):
                for c in range(2):
                    act.wait_ge(g_full, 2 * k + (c + 1))
                    nc.scalar.copy(hT_hi[:, NB * c:NB * c + NB], ps[:, 2 + c, :]).then_inc(g_hi, 1)

            gather_hi(0)
            nc.scalar.activation(warm[:, 6:7], eps[:], ACT.Silu).then_inc(warm_done, 1)
            act.wait_ge(njobs_ready, 1)
            n_jobs = act.value_load(njobs_i[0:1, 0:1], min_val=NE, max_val=2 * NE)

            def job(j, l16, u42, u7, turns, next_job, beside=()):
                def split(i):
                    s = MOE0 + i
                    act.wait_ge(w_used, u42 + (s - SPL + 1))
                    if i in beside:
                        r = beside.index(i)
                        act.wait_ge(spare_landed[r], 16 * len(spare[r]))
                        dst, k = wblock(whi, s, SPL, 4), 0
                        for view in spare[r]:
                            n = view.shape[1]
                            ins = nc.scalar.copy(dst[:, k:k + n, :], view)
                            k += n
                        ins.then_inc(hi_ready, 1)
                        return
                    skipped = turns + sum(i > k and (i - k) % RAW == 0 for k in beside)
                    act.wait_ge(raw_landed[s % RAW], l16 + 16 * (s // RAW + 1 - skipped))
                    nc.scalar.copy(whi[:, s % SPL, :], raw[:, s % RAW, :]).then_inc(hi_ready, 1)

                def silu(n):
                    act.wait_ge(w_used, u42 + (MOE0 + (4 if n == 0 else 6 * n + 2)))
                    nc.scalar.activation(ho[:, 0, :], ps[:, 0, :], ACT.Silu).then_inc(silu_done, 1)

                def hiT(n):
                    act.wait_ge(aT_full, u7 + (2 * NSTEP + n + 1))
                    nc.scalar.copy(aT_hi[:, 0:NB], ps[:, 4, :]).then_inc(aT_hi_done, 1)

                for i in range(3, 6):
                    split(i)
                silu(0)
                for n in range(1, NSTEP):
                    s = 6 * n - 2
                    split(s + 2)
                    hiT(n - 1)
                    if n == 2:
                        act.wait_ge(selT_full, j + 1)
                        nc.scalar.copy(selT[:], ps[:, 5, 0:SEQ]).then_inc(selT_ready, 1)
                    split(s + 3)
                    split(s + 4)
                    split(s + 5)
                    silu(n)
                    split(s + 6)
                    split(s + 7)
                hiT(NSTEP - 1)
                gather_hi(j + 1)
                with next_job():
                    split(FF)
                    split(FF + 1)
                for c in range(2):
                    act.wait_ge(w_used, u42 + (MOE0 + FF - 1 + c))
                    nc.scalar.copy(os_hi[:, NB * c:NB * c + NB], ps[:, 6 + c, :]).then_inc(yj_hi, 1)
                with next_job():
                    split(FF + 2)

            T16 = 16 * FF // RAW
            with act.Fori(0, AHEAD) as j:
                job(j, act.snap(j * T16), act.snap(j * FF), act.snap(j * NSTEP), 0, always)
            job(AHEAD, AHEAD * T16, AHEAD * FF, AHEAD * NSTEP, 0, always, BESIDE)
            with act.Fori(AHEAD + 1, n_jobs) as j:
                job(j, act.snap(j * T16), act.snap(j * FF), act.snap(j * NSTEP), 1, lambda: act.If(j + 1 < n_jobs))
            norm_std(4, lambda t: act.wait_ge(scat_added, n_jobs * 4 + (3 + t)))

        @block.gpsimd
        def _(pool):
            nc.gpsimd.memset(eps[:], EPS).then_inc(init_done, 1)
            nc.gpsimd.memset(selT[:].bitcast(F32), 0.0).then_inc(init_done, 1)
            pool.wait_ge(const_landed, 16 * 7)
            tmp_a = h[:, 0, 0:AW].rearrange("p (h d) -> p h d", d=HD)
            tmp_b = h[:, 1, 0:AW].rearrange("p (h d) -> p h d", d=HD)
            half = HD // 2
            step = 0
            for L in range(2):
                for i in range(4):
                    part, t = divmod(i, 2)
                    pool.wait_ge(proj_evac, NPROD * L + (6 if part == 0 else 8))
                    t_in = qg[:, t, AW * part:AW * part + AW].rearrange("p (h d) -> p h d", d=HD)
                    nh = AW // HD
                    cos = rope[:, t, 0:1, :].broadcast_to([P, nh, HD])
                    nsin = rope[:, t, 1:2, 0:half].broadcast_to([P, nh, half])
                    psin = rope[:, t, 1:2, half:HD].broadcast_to([P, nh, half])
                    if step:
                        pool.wait_ge(rope_done, 4 * L + i)
                    nc.gpsimd.tensor_tensor(tmp_a, t_in, cos, ALU.mult).then_inc(rope_step, 1)
                    nc.gpsimd.tensor_tensor(tmp_b[:, :, 0:half], t_in[:, :, half:HD], nsin, ALU.mult) \
                        .then_inc(rope_step, 1)
                    nc.gpsimd.tensor_tensor(tmp_b[:, :, half:HD], t_in[:, :, 0:half], psin, ALU.mult) \
                        .then_inc(rope_step, 1)
                    step += 3
                    pool.wait_ge(rope_step, step)
                    nc.gpsimd.tensor_tensor(t_in, tmp_a, tmp_b, ALU.add).then_inc(rope_done, 1)
            pool.wait_ge(pv_full, 16)
            nc.gpsimd.memset(ones, 1.0).then_inc(init_done, 1)
            nc.gpsimd.memset(comb[:, :, 0:1], 0.0).then_inc(init_done, 1)
            pool.wait_ge(w_used, MIX1 + 22)
            nc.gpsimd.memset(os_hi[:].bitcast(F32), 0.0).then_inc(init_done, 1)
            for c in range(2):
                nc.gpsimd.memset(os_lo[:, NB * c:NB * c + NB].bitcast(F32), 0.0).then_inc(yj_lo, 1)

        @block.vector
        def _(dve):
            def split_static(b):
                dve.wait_ge(hi_ready, b + 1)
                nc.vector.tensor_tensor(wlo[:, b % SPL, :], raw[:, b % RAW, :],
                                        whi[:, b % SPL, :].bitcast(F32), ALU.subtract).then_inc(lo_ready, 1)

            def split_loop(s, add):
                dve.wait_ge(hi_ready, add + (s + 1))
                nc.vector.tensor_tensor(wlo[:, s % SPL, :], raw[:, s % RAW, :],
                                        whi[:, s % SPL, :].bitcast(F32), ALU.subtract).then_inc(lo_ready, 1)

            def norm(N, K=None, tiles=range(NT), before_lo=lambda: None):
                dve.wait_ge(gain_landed, 16 * N + 16)
                for t in tiles:
                    i = 2 * N + t
                    dve.wait_ge(std_ready, i + 1)
                    nc.vector.reciprocal(rstd[:, i:i + 1], std[:, i:i + 1]).then_inc(rstd_ready, 1)
                    dve.wait_ge(rstd_ready, i + 1)
                    for c in range(2):
                        cols = slice(NB * c, NB * c + NB)
                        nc.vector.scalar_tensor_tensor(h[:, t, cols], x[:, t, cols], rstd[:, i:i + 1], gain[:, cols],
                                                       ALU.mult, ALU.mult).then_inc(h_ready, 1)
                    before_lo()
                    if K is not None:
                        rows_T_lo(K, (2 * t, 2 * t + 1))

            def rows_T_lo(K, places, by_half=False):
                for r in places:
                    t, c = (r % 2, r // 2) if by_half else (r // 2, r % 2)
                    dve.wait_ge(hT_hi_done, 4 * K + r + 1)
                    view = lambda buf: buf.rearrange("p (k s) -> p k s", k=KD)[:, 4 * c:4 * c + 4, P * t:P * t + P]
                    nc.vector.tensor_tensor(view(hT_lo[:, :]), ps[:, 4 + r % 2, :].rearrange("p (k s) -> p k s", k=4),
                                            view(hT_hi[:, :].bitcast(F32)), ALU.subtract).then_inc(hT_lo_done, 1)

            def mixer(L):
                base = 0 if L == 0 else MIX1

                def split(m):
                    split_static(base + m)

                def row_max(u):
                    t = u // HG
                    dve.wait_ge(sc_full, 8 * L + u + 1)
                    if 8 * L + u >= 2:
                        dve.wait_ge(p_ready, 8 * L + u - 1)
                    nc.vector.tensor_tensor_reduce(s_sb[u % 2], ps[:, 6 + u % 2, :], mask[:, SEQ * t:SEQ * t + KEYS],
                                                   1.0, -3.0e38, ALU.add, ALU.max, mx[:, u % 2:u % 2 + 1]) \
                        .then_inc(sc_used, 1)
                    dve.wait_ge(sc_used, 8 * L + u + 1)
                    nc.vector.tensor_scalar(nmx[:, u % 2:u % 2 + 1], mx[:, u % 2:u % 2 + 1], -QS, None, ALU.mult) \
                        .then_inc(nmx_ready, 1)

                def copy_pT(u):
                    dve.wait_ge(pT_full, 8 * L + u + 1)
                    if 8 * L + u >= 2:
                        dve.wait_ge(pv_full, 8 * L + u - 1)
                    nc.vector.tensor_copy(pT[u % 2], ps[:, 4 + u % 2, :]).then_inc(pT_evac, 1)

                def normalise(u):
                    t, j = divmod(u, HG)
                    i = 8 * L + u
                    nc.vector.reciprocal(rden[:, i:i + 1], den[:, i:i + 1]).then_inc(rden_ready, 1)
                    dve.wait_ge(pv_full, i + 1)
                    dve.wait_ge(rden_ready, i + 1)
                    nc.vector.tensor_scalar(o[:, t, HD * j:HD * j + HD], pv_out(u),
                                            rden[:, i:i + 1], None, ALU.mult).then_inc(o_done, 1)

                if L == 0:
                    dve.wait_ge(x_landed[0], 32)
                    norm(0, 0, (0,))
                    for half, hi_done, signal in ((slice(0, BLK // 2), half0_hi, half0_lo),
                                                  (slice(BLK // 2, BLK), hi_ready, lo_ready)):
                        dve.wait_ge(hi_done, 1)
                        nc.vector.tensor_tensor(wlo[:, 0, half], raw[:, 0, half], whi[:, 0, half].bitcast(F32),
                                                ALU.subtract).then_inc(signal, 1)
                    dve.wait_ge(x_landed[1], 32)
                    norm(0, 0, (1,), lambda: split(1))
                else:
                    norm(2, 3, (0,))
                    dense_tail_add(1)
                    split(1)
                    norm(2, 3, (1,))
                for n in range(5):
                    split(2 * n + 2)
                    split(2 * n + 3)
                    if n == 2:
                        for g in range(FG):
                            dve.wait_ge(fa_full, FG * L + g + 1)
                            nc.vector.tensor_copy(fab[:, g, :], ps[:, 6 + g % 2, :]).then_inc(fa_evac, 1)
                    if n == 3:
                        for i in range(2):
                            dve.wait_ge(fb_hi, 2 * L + i + 1)
                            nc.vector.tensor_tensor(aT_lo[:, NB * i:NB * i + NB], ps[:, 6 + i, :],
                                                    aT_hi[:, NB * i:NB * i + NB].bitcast(F32), ALU.subtract) \
                                .then_inc(fb_lo, 1)
                dve.wait_ge(const_landed, 16 * 7)
                for i in range(9):
                    split(12 + i)
                    if i < 8:
                        row_max(i)
                    if i >= 1:
                        copy_pT(i - 1)
                    if i >= 2:
                        normalise(i - 2)
                normalise(7)
                split(21)
                dve.wait_ge(oT_hi, L + 1)
                nc.vector.tensor_tensor(os_lo[:, 0:NB], ps[:, 4, :], os_hi[:, 0:NB].bitcast(F32), ALU.subtract) \
                    .then_inc(oT_lo, 1)

                def zf_half(c, tiles=range(NT)):
                    for t in tiles:
                        nc.vector.tensor_tensor(h[:, t, NB * c:NB * c + NB], ps[:, 2 * t + c, :],
                                                qg[:, t, NB * c:NB * c + NB], ALU.mult).then_inc(zf_done, 1)

                def z_half(c):
                    for t in range(NT):
                        i = 4 * L + 2 * c + t
                        if c == 1:
                            dve.wait_ge(z_ready, i - 1)
                        nc.vector.tensor_tensor(ho[:, t, :], ps[:, 4 + 2 * c + t, :],
                                                qg[:, t, D + NB * c:D + NB * c + NB], ALU.mult).then_inc(za_done, 1)
                        dve.wait_ge(za_done, i + 1)
                        dve.wait_ge(zf_done, i + 1)
                        nc.vector.tensor_tensor(h[:, t, NB * c:NB * c + NB], h[:, t, NB * c:NB * c + NB],
                                                ho[:, t, :], ALU.add).then_inc(z_ready, 1)

                K = 1 if L == 0 else 4
                dve.wait_ge(w_used, base + 21)
                zf_half(0)
                zf_half(1, (0,))
                split(22)
                dve.wait_ge(ya_half, L + 1)
                z_half(0)
                rows_T_lo(K, (0,), by_half=True)
                zf_half(1, (1,))
                rows_T_lo(K, (1,), by_half=True)
                split(23)
                dve.wait_ge(w_used, base + 22)
                z_half(1)
                split(24)
                rows_T_lo(K, (2, 3), by_half=True)
                split(25)
                split(26)
                mixer_add(L, 0)

            def mixer_add(L, t):
                if t == 0:
                    dve.wait_ge(xo_half, L + 1)
                else:
                    dve.wait_ge(w_used, (MIX if L == 0 else MIX1 + MIX))
                for c in range(2):
                    nc.vector.tensor_tensor(x[:, t, NB * c:NB * c + NB], x[:, t, NB * c:NB * c + NB],
                                            ps[:, 2 * t + c, :], ALU.add).then_inc(x_done, 1)
                dve.wait_ge(x_done, 4 * L + 2 * t + 2)

            def dense_tail_add(t):
                for c in range(2):
                    if t == 0:
                        dve.wait_ge(y_full, 2 * NSTEP - 2 + c + 1)
                    else:
                        dve.wait_ge(w_used, MIX1 - 1 + c)
                    nc.vector.tensor_tensor(x[:, t, NB * c:NB * c + NB], x[:, t, NB * c:NB * c + NB],
                                            ps[:, 6 + c, :], ALU.add).then_inc(y_added, 1)
                dve.wait_ge(y_added, 4 * NSTEP - 4 + 2 * t + 2)

            mixer(0)

            norm(1, 2, (0,))
            mixer_add(0, 1)
            split_static(DENSE0 + 1)
            norm(1, 2, (1,))

            def dense_mul(k2, k):
                for t in range(NT):
                    dve.wait_ge(silu_done, k2 + (t + 1))
                    nc.vector.tensor_tensor(ho[:, t, :], ho[:, t, :], ps[:, 2 + t, :], ALU.mult) \
                        .then_inc(act_ready, 1)

            def dense_loT(before_step):
                for t in range(NT):
                    dve.wait_ge(aT_hi_done, before_step + (t + 1))
                    nc.vector.tensor_tensor(aT_lo[:, NB * t:NB * t + NB], ps[:, 4 + t, :],
                                            aT_hi[:, NB * t:NB * t + NB].bitcast(F32), ALU.subtract) \
                        .then_inc(aT_lo_done, 1)

            def dense_add(k2, used, c):
                for t in range(NT):
                    if t == 0:
                        dve.wait_ge(y_full, k2 + (c + 1))
                    else:
                        dve.wait_ge(w_used, used)
                    nc.vector.tensor_tensor(x[:, t, NB * c:NB * c + NB], x[:, t, NB * c:NB * c + NB],
                                            ps[:, 6 + t, :], ALU.add).then_inc(y_added, 1)

            for i in range(2, 6):
                split_static(DENSE0 + i)
            dense_mul(0, 0)
            dense_loT(0)
            with dve.Fori(0, NSTEP - 1) as n:
                for i in range(2, 6):
                    split_loop(DENSE0 + 4 + i, 6 * n)
                dense_mul(2 * n + 2, n)
                dense_add(n * 2, n * 6 + (DENSE0 + 9), 0)
                split_loop(DENSE0 + 4 + 6, 6 * n)
                split_loop(DENSE0 + 4 + 7, 6 * n)
                dense_add(n * 2, n * 6 + (DENSE0 + 10), 1)
                dense_loT(n * 2 + 2)
                dve.wait_ge(y_added, 4 * n + 4)
            split_static(MIX1)
            dense_tail_add(0)
            mixer(1)

            norm(3, tiles=(0,))
            mixer_add(1, 1)
            norm(3, tiles=(1,))
            steps = [0]

            def chain(ins):
                steps[0] += 1
                ins.then_inc(route_step, 1)
                dve.wait_ge(route_step, steps[0])

            V = nc.vector
            lg, c1, one1, l2, c2, one2, msk, cmb = (rt[:, :, i, :] for i in range(8))
            m1, i1, dlt, e21, m2, i2, sm, wa = (r1[:, :, i:i + 1] for i in range(8))
            rev = iota[:, P:P + NE]
            rev2 = rev.rearrange("p (a e) -> p a e", a=1).broadcast_to([P, NT, NE])
            wide = lambda a: a.broadcast_to([P, NT, NE])

            dve.wait_ge(logit_full, 1)
            chain(V.tensor_tensor(lg, ps[:, 6:8, 0:NE],
                                  rb[:, :].rearrange("p (a e) -> p a e", a=1).broadcast_to([P, NT, NE]), ALU.add))

            def first_max(src, m, cand, idx, one):
                chain(V.tensor_reduce(m, src, AX_X, ALU.max))
                V.scalar_tensor_tensor(cand[:, 0, :], src[:, 0, :], m[:, 0, :], rev, ALU.is_ge, ALU.mult) \
                    .then_inc(route_step, 1)
                steps[0] += 1
                chain(V.scalar_tensor_tensor(cand[:, 1, :], src[:, 1, :], m[:, 1, :], rev, ALU.is_ge, ALU.mult))
                chain(V.tensor_reduce(idx, cand, AX_X, ALU.max))
                chain(V.tensor_tensor(one, rev2, wide(idx), ALU.is_equal))

            first_max(lg, m1, c1, i1, one1)
            chain(V.scalar_tensor_tensor(l2, one1, -3.0e38, lg, ALU.mult, ALU.add))
            first_max(l2, m2, c2, i2, one2)
            V.tensor_tensor(msk, one1, one2, ALU.add).then_inc(mask_ready, 1)
            V.tensor_tensor(dlt, m2, m1, ALU.subtract).then_inc(exp_ready, 1)
            split_static(MOE0 + 1)
            dve.wait_ge(rank_full, 1)
            V.tensor_reduce(njobs_f[:, 0:1], ps[:, 2, 32:32 + NE], AX_X, ALU.max).then_inc(count_max, 1)
            dve.wait_ge(mask_ready, 1)
            chain(V.scalar_tensor_tensor(pos[:, :, 0:NE], ps[:, 2:4, 16:16 + NE], 1000.0, msk, ALU.add, ALU.mult))

            def build_sel(col):
                for t in range(NT):
                    V.tensor_scalar(sel[:, t, :], iota[:, 0:P], col(pos, t), None, ALU.is_equal).then_inc(sel_ready, 1)

            build_sel(lambda a, t: a[:, t, 0:1])
            chain(V.tensor_scalar(pos[:, :, NE:2 * NE], pos[:, :, 0:NE], -float(P), None, ALU.add))
            chain(V.memset(pos[:, :, 2 * NE:2 * NE + 1], -1.0))
            dve.wait_ge(count_max, 1)
            chain(V.tensor_scalar(njobs_f[:, 1:2], njobs_f[:, 0:1], P + 0.5, float(NE), ALU.is_gt, ALU.mult))
            chain(V.tensor_scalar(njobs_f[:, 2:3], njobs_f[:, 1:2], float(NE), None, ALU.add))
            V.tensor_copy(njobs_i[:], njobs_f[:, 2:3]).then_inc(njobs_ready, 1)

            def gather_lo(k):
                for c in range(2):
                    dve.wait_ge(g_hi, 2 * k + (c + 1))
                    V.tensor_tensor(hT_lo[:, NB * c:NB * c + NB], ps[:, 2 + c, :],
                                    hT_hi[:, NB * c:NB * c + NB].bitcast(F32), ALU.subtract).then_inc(g_lo, 1)

            split_static(MOE0 + 2)
            dve.wait_ge(exp_ready, 2)
            chain(V.tensor_scalar(sm, e21, 1.0, None, ALU.add))
            chain(V.reciprocal(wa, sm))
            chain(V.tensor_tensor(cmb, one2, wide(e21), ALU.mult))
            chain(V.tensor_tensor(cmb, cmb, one1, ALU.add))
            chain(V.tensor_tensor(cmb, cmb, wide(wa), ALU.mult))
            for r in range(2):
                chain(V.tensor_copy(comb[:, :, 1 + NE * r:1 + NE * r + NE], cmb))
            gather_lo(0)
            dve.wait_ge(njobs_ready, 1)
            n_jobs = dve.value_load(njobs_i[0:1, 0:1], min_val=NE, max_val=2 * NE)

            def scatter_add(k4, job):
                for c in range(2):
                    for t in range(NT):
                        i = 2 * c + t
                        dve.wait_ge(scat_full, k4 + (i + 1))
                        V.scalar_tensor_tensor(x[:, t, NB * c:NB * c + NB], ps[:, 2 + t, :],
                                               comb[:, t, bass.ds(job, 1)],
                                               x[:, t, NB * c:NB * c + NB], ALU.mult, ALU.add) \
                            .then_inc(scat_added, 1)

            def job(j, u42, u7, u4, next_job, beside=()):
                def split(i):
                    if i not in beside:
                        split_loop(MOE0 + i, u42)
                        return
                    s = MOE0 + i
                    dve.wait_ge(hi_ready, u42 + (s + 1))
                    hi, lo = (wblock(buf, s, SPL, 4) for buf in (whi, wlo))
                    k = 0
                    for view in spare[beside.index(i)]:
                        part = slice(k, k + view.shape[1])
                        ins = V.tensor_tensor(lo[:, part, :], view, hi[:, part, :].bitcast(F32), ALU.subtract)
                        k = part.stop
                    ins.then_inc(lo_ready, 1)

                def mul(n):
                    dve.wait_ge(silu_done, u7 + (2 * NSTEP + n + 1))
                    V.tensor_tensor(ho[:, 0, :], ho[:, 0, :], ps[:, 1, :], ALU.mult).then_inc(act_ready, 1)

                def loT(n):
                    dve.wait_ge(aT_hi_done, u7 + (2 * NSTEP + n + 1))
                    V.tensor_tensor(aT_lo[:, 0:NB], ps[:, 4, :], aT_hi[:, 0:NB].bitcast(F32), ALU.subtract) \
                        .then_inc(aT_lo_done, 1)

                for i in range(3, 6):
                    split(i)
                mul(0)
                scatter_add(u4, j)
                for n in range(1, NSTEP):
                    s = 6 * n - 2
                    split(s + 2)
                    loT(n - 1)
                    split(s + 3)
                    split(s + 4)
                    split(s + 5)
                    mul(n)
                    if n == 3:
                        dve.wait_ge(selT_full, j + 1)
                        build_sel(lambda a, t: a[:, t, bass.ds(j + 1, 1)])
                    split(s + 6)
                    split(s + 7)
                loT(NSTEP - 1)
                gather_lo(j + 1)
                with next_job():
                    split(FF)
                    split(FF + 1)
                for c in range(2):
                    dve.wait_ge(yj_hi, j * 2 + (c + 1))
                    V.tensor_tensor(os_lo[:, NB * c:NB * c + NB], ps[:, 6 + c, :],
                                    os_hi[:, NB * c:NB * c + NB].bitcast(F32), ALU.subtract).then_inc(yj_lo, 1)
                with next_job():
                    split(FF + 2)
                dve.wait_ge(scat_added, u4 + 4)

            dve.wait_ge(init_done, 4)
            with dve.Fori(0, AHEAD) as j:
                job(j, dve.snap(j * FF), dve.snap(j * NSTEP), dve.snap(j * 4), always)
            job(AHEAD, AHEAD * FF, AHEAD * NSTEP, AHEAD * 4, always, BESIDE)
            with dve.Fori(AHEAD + 1, n_jobs) as j:
                job(j, dve.snap(j * FF), dve.snap(j * NSTEP), dve.snap(j * 4), lambda: dve.If(j + 1 < n_jobs))
            scatter_add(dve.snap(n_jobs * 4), n_jobs)
            dve.wait_ge(scat_added, n_jobs * 4 + 4)
            norm(4)

        @block.tensor
        def _(pe):
            mm = nc.tensor.matmul

            def three(dst, a_hi, a_lo, b_hi, b_lo, start, stop):
                mm(dst, a_hi, b_hi, start=start, stop=False)
                mm(dst, a_lo, b_hi, start=False, stop=False)
                return mm(dst, a_hi, b_lo, start=False, stop=stop)

            def rows_T(K, r, t, c, src):
                if r >= 2:
                    pe.wait_ge(hT_lo_done, 4 * K + r - 1)
                for k in range(4):
                    last = nc.tensor.transpose(ps[:, 4 + r % 2, P * k:P * k + P],
                                               src[:, t, P * (4 * c + k):P * (4 * c + k) + P], ident[:])
                last.then_inc(hT_full, 1)

            def normed_T(K, N, t):
                for c in range(2):
                    pe.wait_ge(h_ready, 4 * N + 2 * t + c + 1)
                    rows_T(K, 2 * t + c, t, c, h)

            def mixer(L, tile0_T):
                base = 0 if L == 0 else MIX1

                K0 = 0 if L == 0 else 3

                def proj_first():
                    for t in range(NT):
                        for m in range(2):
                            b = base + m
                            hi, lo = wblock(whi, b, SPL, 4), wblock(wlo, b, SPL, 4)
                            if L == 0 and m == 0 and t == 0:
                                normed_T(0, 0, 0)
                            by_half = L == 0 and m == 0 and t == 0
                            if by_half:
                                pe.wait_ge(half0_lo, 1)
                            elif t == 0:
                                pe.wait_ge(lo_ready, b + 1)
                            pe.wait_ge(hT_lo_done, 4 * K0 + 2 * t + m + 1)
                            for k in range(4):
                                if by_half and k == 2:
                                    pe.wait_ge(lo_ready, 1)
                                a = SEQ * (4 * m + k) + P * t
                                ins = three(ps[:, t, :], hT_hi[:, a:a + P], hT_lo[:, a:a + P],
                                            hi[:, k, :], lo[:, k, :], m == 0 and k == 0, m == 1 and k == 3)
                                if m == 1 and t == 0 and k == 1:
                                    normed_T(K0, 2 * L, 1)
                            if t == 1:
                                ins.then_inc(w_used, 1)

                def proj_block(m, n, between_tiles=lambda: None):
                    b = base + m
                    chunks = 8 if m == 10 else 4
                    cols = 256 if m == 10 else NB
                    first = m == 10 or (m % 2 == 0 if m < 10 else m % 2 == 1)
                    last_half = m == 10 or not first
                    k0 = 0 if first else 4
                    hi, lo = wblock(whi, b, SPL, chunks), wblock(wlo, b, SPL, chunks)
                    for t in range(NT):
                        if t == 0:
                            pe.wait_ge(lo_ready, b + 1)
                        else:
                            between_tiles()
                        q = 2 * n + t
                        if first and q >= 4:
                            pe.wait_ge(proj_evac, NPROD * L + (q - 3 if q < 12 else q - 1))
                        for k in range(chunks):
                            a = SEQ * (k0 + k) + P * t
                            ins = three(ps[:, proj_bank(q), 0:cols], hT_hi[:, a:a + P], hT_lo[:, a:a + P],
                                        hi[:, k, :], lo[:, k, :], first and k == 0, last_half and k == chunks - 1)
                    ins.then_inc(w_used, 1)

                def fourier_a():
                    pe.wait_ge(proj_evac, NPROD * L + 2)
                    pe.wait_ge(dft_landed, 16 * L + 16)
                    pe.wait_ge(const_landed, 16 * 7)
                    for g in range(FG):
                        if g >= 2:
                            pe.wait_ge(fa_evac, FG * L + g - 1)
                        for t in range(NT):
                            ins = mm(ps[:, 6 + g % 2, :], ho[:, t, P * g:P * g + P], dftpos[:, t, :],
                                     start=t == 0, stop=t == NT - 1)
                        ins.then_inc(fa_full, 1)

                def fourier_b():
                    for i in range(2):
                        pe.wait_ge(fa_evac, FG * L + 4)
                        for g in (2 * i, 2 * i + 1):
                            dst = ps[:, 6 + i, SEQ * (g % 2):SEQ * (g % 2) + SEQ]
                            mm(dst, dftch[:, 0, :], fab[:, g, 0:SEQ], start=True, stop=False)
                            ins = mm(dst, dftch[:, 1, :], fab[:, g, SEQ:2 * SEQ], start=False, stop=True)
                        ins.then_inc(fb_full, 1)

                def qk_T(i):
                    part, t = divmod(i, 2)
                    pe.wait_ge(rope_done, 4 * L + i + 1)
                    if i:
                        pe.wait_ge(qkT_evac, 4 * L + i)
                    for c in range(6):
                        a = AW * part + P * c
                        ins = nc.tensor.transpose(psT[:, P * c:P * c + P], qg[:, t, a:a + P], ident[:])
                    ins.then_inc(qkT_full, 1)

                def key_blocks(t):
                    band, dil = [(0, 0), (0, 1)], [(1, t), (2, t)]
                    return band + dil if t == 0 else dil + band

                def scores(u):
                    t, j = divmod(u, HG)
                    if u == 0:
                        pe.wait_ge(qkT_evac, 4 * L + 4)
                        pe.wait_ge(fb_lo, 2 * L + 2)
                    elif u >= 2:
                        pe.wait_ge(sc_used, 8 * L + u - 1)
                    blocks = key_blocks(t)
                    for i, (g, kt) in enumerate(blocks):
                        if g == 0 and kt == 1:
                            continue
                        n = SEQ if g == 0 else P
                        head = HG * g + j
                        c, p0 = head // 2, HD * (head % 2)
                        ins = mm(ps[:, 6 + u % 2, P * i:P * i + n], qkTc[p0:p0 + HD, c, P * t:P * t + P],
                                 qkTc[p0:p0 + HD, 6 + c, P * kt:P * kt + n], start=True, stop=True)
                    ins.then_inc(sc_full, 1)

                def prob_T(u):
                    pe.wait_ge(p_ready, 8 * L + u + 1)
                    if u >= 2:
                        pe.wait_ge(pT_evac, 8 * L + u - 1)
                    for c in range(KEYS // P):
                        ins = nc.tensor.transpose(ps[:, 4 + u % 2, P * c:P * c + P], p_sb[u % 2][:, P * c:P * c + P],
                                                  ident[:])
                    ins.then_inc(pT_full, 1)

                def prob_v(u):
                    t, j = divmod(u, HG)
                    pe.wait_ge(pT_evac, 8 * L + u + 1)
                    if u < 2:
                        pe.wait_ge(proj_evac, NPROD * L + 11 + u)
                    elif u < 6:
                        pe.wait_ge(o_done, 8 * L + u - 1)
                    blocks = key_blocks(t)
                    for c, (g, kt) in enumerate(blocks):
                        head = HG * g + j
                        ins = mm(pv_out(u), pT[u % 2][:, P * c:P * c + P], v[:, kt, HD * head:HD * head + HD],
                                 start=c == 0, stop=c == len(blocks) - 1)
                    ins.then_inc(pv_full, 1)

                proj_first()
                for m in range(2, 11):
                    if m >= 8:
                        qk_T(m - 8)
                    proj_block(m, m // 2)
                    if m == 5:
                        fourier_a()
                    if m == 7:
                        fourier_b()
                def attention_T():
                    pe.wait_ge(o_done, 8 * L + 8)
                    for c in range(2):
                        for t in range(NT):
                            ins = nc.tensor.transpose(ps[:, 4, SEQ * c + P * t:SEQ * c + P * t + P],
                                                      o[:, t, P * c:P * c + P], ident[:])
                    ins.then_inc(oT_full, 1)

                qk_T(3)
                for i in range(10):
                    if 1 <= i < 8:
                        scores(i)
                    if 1 <= i <= 8:
                        prob_T(i - 1)
                    if i >= 2:
                        prob_v(i - 2)
                    if i < 8:
                        proj_block(11 + i, 6 + i // 2, (lambda: scores(0)) if i == 0 else (lambda: None))
                    else:
                        b = base + 11 + i
                        if i == 8:
                            pe.wait_ge(proj_evac, NPROD * L + 20)
                            pe.wait_ge(o_done, 8 * L + 6)
                        pe.wait_ge(lo_ready, b + 1)
                        hi, lo = wblock(whi, b, SPL, 2), wblock(wlo, b, SPL, 2)
                        for t in range(NT):
                            if i == 9 and t == 1:
                                attention_T()
                            for c in range(2):
                                for k in range(2):
                                    a = SEQ * (2 * (i - 8) + k) + P * t
                                    ins = three(ps[:, 2 * t + c, :], aT_hi[:, a:a + P], aT_lo[:, a:a + P],
                                                hi[:, k, NB * c:NB * c + NB], lo[:, k, NB * c:NB * c + NB],
                                                i == 8 and k == 0, i == 9 and k == 1)
                        ins.then_inc(w_used, 1)
                b = base + 21
                pe.wait_ge(oT_lo, L + 1)
                pe.wait_ge(lo_ready, b + 1)
                hi, lo = wblock(whi, b, SPL, 2), wblock(wlo, b, SPL, 2)
                for c in range(2):
                    for t in range(NT):
                        for k in range(2):
                            a = SEQ * k + P * t
                            ins = three(ps[:, 4 + 2 * c + t, :], os_hi[:, a:a + P], os_lo[:, a:a + P],
                                        hi[:, k, NB * c:NB * c + NB], lo[:, k, NB * c:NB * c + NB], k == 0, k == 1)
                    ins.then_inc(ya_half if c == 0 else w_used, 1)
                K = 1 if L == 0 else 4

                def z_T(c):
                    for t in range(NT):
                        pe.wait_ge(z_ready, 4 * L + 2 * c + t + 1)
                        rows_T(K, 2 * c + t, t, c, h)

                z_T(0)
                for i, t in ((0, 0), (0, 1), (1, 0), (1, 1), (2, 0), (3, 0), (2, 1), (3, 1)):
                    b = base + 22 + i
                    if t == 0:
                        pe.wait_ge(lo_ready, b + 1)
                    if i % 2 == 0:
                        pe.wait_ge(hT_lo_done, 4 * K + i + t + 1)
                    hi, lo = wblock(whi, b, SPL, 2), wblock(wlo, b, SPL, 2)
                    for c in range(2):
                        if i == 0:
                            pe.wait_ge(zf_done, 4 * L + 2 * c + t + 1)
                        for k in range(2):
                            a = SEQ * (2 * i + k) + P * t
                            ins = three(ps[:, 2 * t + c, :], hT_hi[:, a:a + P], hT_lo[:, a:a + P],
                                        hi[:, k, NB * c:NB * c + NB], lo[:, k, NB * c:NB * c + NB],
                                        i == 0 and k == 0, i == 3 and k == 1)
                        if i == 3 and t == 1 and c == 0:
                            tile0_T()
                    if i == 3 and t == 0:
                        ins.then_inc(xo_half, 1)
                    elif t == 1:
                        ins.then_inc(w_used, 1)
                    if i == 0 and t == 1:
                        z_T(1)

            pe.wait_ge(ident_landed, 16)
            mixer(0, lambda: normed_T(2, 1, 0))

            def dense_up(s, add, first=False):
                gate = ((0, 0), (1, 0), (0, 1), (1, 1)) if first else ((0, 0), (0, 1), (1, 0), (1, 1))
                for i, t in gate + ((2, 0), (2, 1), (3, 0), (3, 1)):
                    if t == 0:
                        pe.wait_ge(lo_ready, add + (s + i + 1))
                    if first and i <= 1:
                        pe.wait_ge(hT_lo_done, 8 + 2 * t + i + 1)
                    hi, lo = wblock(whi, s + i, SPL, 4), wblock(wlo, s + i, SPL, 4)
                    for k in range(4):
                        a = SEQ * (4 * (i % 2) + k) + P * t
                        ins = three(ps[:, 2 * (i // 2) + t, :], hT_hi[:, a:a + P], hT_lo[:, a:a + P],
                                    hi[:, k, :], lo[:, k, :], i % 2 == 0 and k == 0, i % 2 == 1 and k == 3)
                        if first and i == 1 and t == 0 and k == 1:
                            normed_T(2, 1, 1)
                    if t == 1:
                        ins.then_inc(w_used, 1)

            def dense_down(s, add, steps2, added):
                for c in range(2):
                    pe.wait_ge(lo_ready, add + (s + c + 1))
                    hi, lo = wblock(whi, s + c, SPL, 4), wblock(wlo, s + c, SPL, 4)
                    for t in range(NT):
                        if c == 0:
                            pe.wait_ge(aT_lo_done, steps2 + (1 + t))
                        if c == 1:
                            pe.wait_ge(y_added, added + (t + 1))
                        for k in range(4):
                            a = NB * t + P * k
                            ins = three(ps[:, 6 + t, :], aT_hi[:, a:a + P], aT_lo[:, a:a + P],
                                        hi[:, k, :], lo[:, k, :], k == 0, k == 3)
                        ins.then_inc(y_full if t == 0 else w_used, 1)

            def dense_T(before_step):
                for t in range(NT):
                    pe.wait_ge(act_ready, before_step + (1 + t))
                    for k in range(4):
                        ins = nc.tensor.transpose(ps[:, 4 + t, P * k:P * k + P], ho[:, t, P * k:P * k + P], ident[:])
                    ins.then_inc(aT_full, 1)

            dense_up(DENSE0, 0, first=True)
            dense_T(0)
            with pe.Fori(0, NSTEP - 1) as n:
                n6, n4 = pe.snap(n * 6), pe.snap(n * 4)
                dense_up(DENSE0 + 4, n6)
                with pe.If(n > 0):
                    pe.wait_ge(y_added, n4)
                dense_down(DENSE0 + 8, n6, n * 2, n4)
                dense_T(n * 2 + 2)
            pe.wait_ge(y_added, 4 * NSTEP - 4)
            for t in range(NT):
                pe.wait_ge(aT_lo_done, 2 * NSTEP - 2 + (1 + t))
                for c in range(2):
                    b = DENSE0 + FF - 2 + c
                    if t == 0:
                        pe.wait_ge(lo_ready, b + 1)
                    else:
                        pe.wait_ge(y_added, 4 * NSTEP - 4 + (c + 1))
                    hi, lo = wblock(whi, b, SPL, 4), wblock(wlo, b, SPL, 4)
                    for k in range(4):
                        a = NB * t + P * k
                        ins = three(ps[:, 6 + c, :], aT_hi[:, a:a + P], aT_lo[:, a:a + P],
                                    hi[:, k, :], lo[:, k, :], k == 0, k == 3)
                        if t == 1 and c == 1 and k == 1:
                            normed_T(3, 2, 0)
                    ins.then_inc(y_full if t == 0 else w_used, 1)

            def rout_T(t):
                for c in range(2):
                    r = 2 * t + c
                    pe.wait_ge(h_ready, 12 + r + 1)
                    if r >= 2:
                        pe.wait_ge(rT_evac, r - 1)
                    for k in range(4):
                        ins = nc.tensor.transpose(ps[:, 4 + r % 2, P * k:P * k + P],
                                                  h[:, t, P * (4 * c + k):P * (4 * c + k) + P], ident[:])
                    ins.then_inc(rT_full, 1)

            mixer(1, lambda: rout_T(0))

            for t in range(NT):
                if t == 1:
                    rout_T(1)
                for k in range(KD):
                    if k % 4 == 0:
                        pe.wait_ge(rT_evac, 2 * t + k // 4 + 1)
                    ins = mm(ps[:, 6 + t, 0:NE], routT[:, k, P * t:P * t + P], rw[:, k, :],
                             start=k == 0, stop=k == KD - 1)
            ins.then_inc(logit_full, 1)
            pe.wait_ge(init_done, 4)
            pe.wait_ge(mask_ready, 1)
            msk = [rt[:, t, 6, :] for t in range(NT)]
            mm(ps[:, 2, 16:16 + NE], before[:], msk[0], start=True, stop=True)
            mm(ps[:, 3, 16:16 + NE], ones, msk[0], start=True, stop=False)
            mm(ps[:, 3, 16:16 + NE], before[:], msk[1], start=False, stop=True)
            mm(ps[:, 2, 32:32 + NE], ones, msk[0], start=True, stop=False)
            mm(ps[:, 2, 32:32 + NE], ones, msk[1], start=False, stop=True).then_inc(rank_full, 1)
            def gather(sel_count):
                pe.wait_ge(sel_ready, sel_count)
                for k in range(KD):
                    for t in range(NT):
                        ins = mm(ps23[:, P * k:P * k + P], h[:, t, P * k:P * k + P], sel[:, t, :],
                                 start=t == 0, stop=t == NT - 1)
                    if k % 4 == 3:
                        ins.then_inc(g_full, 1)

            def scatter(c, halves, added):
                pe.wait_ge(yj_lo, halves + (1 + c))
                for t in range(NT):
                    if c == 1:
                        pe.wait_ge(scat_added, added + (t + 1))
                    lhs = selT[:, P * t:P * t + P]
                    mm(ps[:, 2 + t, :], lhs, os_hi[:, NB * c:NB * c + NB], start=True, stop=False)
                    ins = mm(ps[:, 2 + t, :], lhs, os_lo[:, NB * c:NB * c + NB], start=False, stop=True)
                    ins.then_inc(scat_full, 1)

            gather(2)
            pe.wait_ge(njobs_ready, 1)
            n_jobs = pe.value_load(njobs_i[0:1, 0:1], min_val=NE, max_val=2 * NE)
            pe.wait_ge(init_done, 5)
            with pe.Fori(0, n_jobs) as j:
                u42, u7, u4 = pe.snap(j * FF), pe.snap(j * NSTEP), pe.snap(j * 4)

                def up(s, after_first=lambda: None):
                    for i in range(4):
                        if i == 1:
                            after_first()
                        b = MOE0 + s + i
                        pe.wait_ge(lo_ready, u42 + (b + 1))
                        hi, lo = wblock(whi, b, SPL, 4), wblock(wlo, b, SPL, 4)
                        for k in range(4):
                            if s == 0 and i < 2 and k == 0:
                                pe.wait_ge(g_lo, j * 2 + (i + 1))
                            a = P * (4 * (i % 2) + k)
                            ins = three(ps[:, i // 2, :], hT_hi[:, a:a + P], hT_lo[:, a:a + P],
                                        hi[:, k, :], lo[:, k, :], i % 2 == 0 and k == 0, i % 2 == 1 and k == 3)
                        ins.then_inc(w_used, 1)

                def hidden_T(n):
                    pe.wait_ge(act_ready, u7 + (2 * NSTEP + n + 1))
                    for k in range(4):
                        ins = nc.tensor.transpose(ps[:, 4, P * k:P * k + P], ho[:, 0, P * k:P * k + P], ident[:])
                    ins.then_inc(aT_full, 1)

                def down(n, s):
                    pe.wait_ge(aT_lo_done, u7 + (2 * NSTEP + n + 1))
                    for c in range(2):
                        b = MOE0 + s + c
                        pe.wait_ge(lo_ready, u42 + (b + 1))
                        hi, lo = wblock(whi, b, SPL, 4), wblock(wlo, b, SPL, 4)
                        for k in range(4):
                            ins = three(ps[:, 6 + c, :], aT_hi[:, P * k:P * k + P], aT_lo[:, P * k:P * k + P],
                                        hi[:, k, :], lo[:, k, :], n == 0 and k == 0, n == NSTEP - 1 and k == 3)
                        ins.then_inc(w_used, 1)

                up(0)
                scatter(0, j * 2, u4)
                pe.wait_ge(silu_done, u7 + (2 * NSTEP + 1))

                def after_first():
                    hidden_T(0)
                    scatter(1, j * 2, u4)

                for n in range(1, NSTEP):
                    s = 6 * n - 2
                    up(s, after_first if n == 1 else lambda: None)
                    if n == 1:
                        for t in range(NT):
                            ins = nc.tensor.transpose(ps[:, 5, P * t:P * t + P], sel[:, t, :], ident[:])
                        ins.then_inc(selT_full, 1)
                    down(n - 1, s + 4)
                    hidden_T(n)
                pe.wait_ge(scat_added, u4 + 4)
                gather(2 * j + 4)
                down(NSTEP - 1, FF - 2)
            for c in range(2):
                scatter(c, n_jobs * 2, pe.snap(n_jobs * 4))


def _constants():
    import numpy as np
    f = np.float32
    tok = (RES * np.arange(HALF)[None, :] + np.arange(RES)[:, None]).reshape(SEQ)
    s = tok.astype(np.float64)
    ang = 2 * np.pi * np.outer(s, s) / SEQ
    pos = np.concatenate([np.cos(ang), np.sin(ang)], 1) / np.sqrt(SEQ)
    c = np.arange(P, dtype=np.float64)
    angc = 2 * np.pi * np.outer(c, c) / P
    ch = np.stack([np.cos(angc), -np.sin(angc)], 1) / np.sqrt(P)
    no = f(-1e30)
    apart = tok[:, None] - tok[None, :]
    band = np.where(np.abs(apart) <= HD, f(0), no).reshape(NT, P, SEQ)
    dil = [np.where(apart[:P, :P] % d == 0, f(0), no) for d in (4, 16)]
    mask = np.concatenate([band[0], dil[0], dil[1], band[1]], 1).astype(f)
    half = HD // 2
    inv = f(10000.0) ** (-np.arange(half, dtype=f) * f(2.0) / f(HD))
    a = (tok.astype(f)[:, None] * inv[None, :].astype(f)).astype(f)
    co, si = np.cos(a), np.sin(a)
    rope = np.stack([np.concatenate([co, co], 1), np.concatenate([-si, si], 1)], 1)
    rope = rope.reshape(NT, P, 2, HD).transpose(1, 0, 2, 3)
    return {
        "c_ident": np.eye(P, dtype=f),
        "c_dftpos": pos.reshape(NT, P, NB).transpose(1, 0, 2).astype(f),
        "c_dftch": ch.astype(f),
        "c_mask": mask,
        "c_rope": rope.astype(f),
        "c_iota": np.tile(np.concatenate([1000 + np.arange(P), NE - np.arange(NE)]).astype(f), (P, 1)),
        "c_before": np.triu(np.ones((P, P), f), 1),
    }


_INS = ["x", "ln_mix", "w_in", "w_fourier", "w_attn", "w_out", "ln_ffn", "dense_w1", "dense_w3", "dense_w2",
        "router_w", "router_b", "moe_w1", "moe_w3", "moe_w2", "ln_final"]


def kernel(**inputs):
    import numpy as np
    import concourse.bacc as bacc
    from concourse.bass_utils import run_bass_kernel_spmd

    nc = bacc.Bacc("TRN2", target_bir_lowering=False, num_devices=1)
    arrays, args = {}, []
    feeds = {name: np.asarray(inputs[name]) for name in _INS}
    feeds.update(_constants())
    for name, a in feeds.items():
        a = np.ascontiguousarray(a)
        arrays[f"in_{name}"] = a
        args.append(nc.dram_tensor(f"in_{name}", a.shape, mybir.dt.from_np(a.dtype), kind="ExternalInput").ap())
    args.append(nc.dram_tensor("out_0", (1, SEQ, D), F32, kind="ExternalOutput").ap())
    build(nc, *args)
    r = run_bass_kernel_spmd(nc, [arrays], core_ids=[0])
    return r.results[0]["out_0"]
```
